# Optimizing a Trainium2 kernel written in Bass

```python
import jax, jax.numpy as jnp
from jax import lax
import numpy as np

D_MODEL = 2048
BATCH = 1
SEQ = 256
DEPTH = 2

MIX_WIDTH = D_MODEL
EPS = 1e-6
LRU_WIDTH = MIX_WIDTH // 2
LRU_BLOCKS = 8
LRU_BLOCK_W = LRU_WIDTH // LRU_BLOCKS
CONV_W = 4
LRU_C = 8.0
MLSTM_WIDTH = MIX_WIDTH // 2
MLSTM_HEADS = 4
MLSTM_DV = MLSTM_WIDTH // MLSTM_HEADS
MLSTM_DK = MLSTM_DV // 2
MLSTM_QK = MLSTM_HEADS * MLSTM_DK
MLSTM_CHUNK = 128
AB_IN = 2 * LRU_WIDTH + 2 * MLSTM_QK + 2 * MLSTM_WIDTH + 2 * MLSTM_HEADS
SB_HEADS = 16
SB_HEAD_DIM = MIX_WIDTH // SB_HEADS
SB_BLOCK = 128
FFN_HIDDEN = ((8 * D_MODEL // 3 + 255) // 256) * 256

kernel_name = "hybrid_rglru_mlstm_stickbreaking_adaln"

def rmsnorm(x, g):
    xf = x.astype(jnp.float32)
    y = xf * lax.rsqrt(jnp.mean(xf * xf, axis=-1, keepdims=True) + EPS)
    return (y * g.astype(jnp.float32)).astype(x.dtype)

def causal_depthwise_conv(x, w, b):
    C = x.shape[-1]
    y = lax.conv_general_dilated(x, w[:, None, :], window_strides=(1,), padding=[(CONV_W - 1, 0)],
                                 dimension_numbers=("NWC", "WIO", "NWC"), feature_group_count=C)
    return y + b

def _linear_recurrence_combine(e1, e2):
    a1, b1 = e1
    a2, b2 = e2
    return a1 * a2, a2 * b1 + b2

def rglru(x, gate_w, gate_b, lam):
    B, S, _ = x.shape
    xb = x.reshape(B, S, LRU_BLOCKS, LRU_BLOCK_W)
    g = jnp.einsum("bsnd,gnde->gbsne", xb, gate_w).reshape(2, B, S, LRU_WIDTH) + gate_b[:, None, None, :]
    r = jax.nn.sigmoid(g[0])
    i = jax.nn.sigmoid(g[1])
    log_a = LRU_C * r * jax.nn.log_sigmoid(lam)
    a = jnp.exp(log_a)
    u = jnp.sqrt(-jnp.expm1(2.0 * log_a)) * (i * x)
    _, h = lax.associative_scan(_linear_recurrence_combine, (a, u), axis=1)
    return h

def mlstm_chunkwise(q, k, v, ig, fg):
    B, S, H, _ = q.shape
    L = MLSTM_CHUNK
    NC = S // L

    def chunks(t):
        t = t.reshape((B, NC, L, H) + t.shape[3:])
        return jnp.moveaxis(jnp.moveaxis(t, 1, 0), 3, 2)

    qc = chunks(q)
    kc = chunks(k * (MLSTM_DK ** -0.5))
    vc = chunks(v)
    lic = chunks(ig)
    lfc = chunks(jax.nn.log_sigmoid(fg))
    causal = jnp.tril(jnp.ones((L, L), dtype=bool))

    def step(carry, xs):
        C, n, m = carry
        qb, kb, vb, li, lf = xs
        bcum = jnp.cumsum(lf, axis=-1)
        Dm = jnp.where(causal, bcum[..., :, None] - bcum[..., None, :] + li[..., None, :], -jnp.inf)
        m_inter = bcum + m[..., None]
        m_t = jnp.maximum(m_inter, jnp.max(Dm, axis=-1))
        w_intra = jnp.exp(Dm - m_t[..., None])
        w_inter = jnp.exp(m_inter - m_t)
        s = jnp.einsum("bhtd,bhsd->bhts", qb, kb) * w_intra
        num = jnp.einsum("bhts,bhsv->bhtv", s, vb) + w_inter[..., None] * jnp.einsum("bhvd,bhtd->bhtv", C, qb)
        den = jnp.sum(s, axis=-1) + w_inter * jnp.einsum("bhd,bhtd->bht", n, qb)
        h = num / jnp.maximum(jnp.abs(den), jnp.exp(-m_t))[..., None]
        b_last = bcum[..., -1]
        gk = b_last[..., None] - bcum + li
        m_new = jnp.maximum(b_last + m, jnp.max(gk, axis=-1))
        decay = jnp.exp(b_last + m - m_new)
        wk = jnp.exp(gk - m_new[..., None])
        C_new = decay[..., None, None] * C + jnp.einsum("bhs,bhsv,bhsd->bhvd", wk, vb, kb)
        n_new = decay[..., None] * n + jnp.einsum("bhs,bhsd->bhd", wk, kb)
        return (C_new, n_new, m_new), h

    init = (jnp.zeros((B, H, MLSTM_DV, MLSTM_DK), jnp.float32),
            jnp.zeros((B, H, MLSTM_DK), jnp.float32),
            jnp.zeros((B, H), jnp.float32))
    _, hs = lax.scan(step, init, (qc, kc, vc, lic, lfc))
    return jnp.transpose(hs, (1, 0, 3, 2, 4)).reshape(B, S, H, MLSTM_DV)

def rglru_mlstm_mixer(h, w_in, w_out, conv_w, conv_b, gate_w, gate_b, lam, m_gate_b, m_norm_g):
    B, S, _ = h.shape
    f32 = jnp.float32
    proj = (h @ w_in).astype(f32)
    cuts = np.cumsum([LRU_WIDTH, LRU_WIDTH, MLSTM_QK, MLSTM_QK, MLSTM_WIDTH, MLSTM_WIDTH, MLSTM_HEADS])
    xa, ya, q, k, v, o, ig, fg = jnp.split(proj, cuts, axis=-1)
    xa = causal_depthwise_conv(xa, conv_w.astype(f32), conv_b.astype(f32))
    out_a = rglru(xa, gate_w.astype(f32), gate_b.astype(f32), lam.astype(f32)) * jax.nn.gelu(ya)
    mgb = m_gate_b.astype(f32)
    hb = mlstm_chunkwise(q.reshape(B, S, MLSTM_HEADS, MLSTM_DK), k.reshape(B, S, MLSTM_HEADS, MLSTM_DK),
                         v.reshape(B, S, MLSTM_HEADS, MLSTM_DV), ig + mgb[0], fg + mgb[1])
    hb = hb * lax.rsqrt(jnp.mean(hb * hb, axis=-1, keepdims=True) + EPS)
    hb = hb * m_norm_g.astype(f32).reshape(MLSTM_HEADS, MLSTM_DV)
    out_b = hb.reshape(B, S, MLSTM_WIDTH) * jax.nn.sigmoid(o)
    mix = jnp.concatenate([out_a, out_b], axis=-1).astype(h.dtype)
    return mix @ w_out

def _stick_breaking_block(qb, kp, vp, start):
    z = jnp.einsum("bhtd,bhsd->bhts", qb, kp) * (SB_HEAD_DIM ** -0.5)
    t_idx = start + jnp.arange(qb.shape[2])
    s_idx = jnp.arange(kp.shape[2])
    mask = s_idx[None, :] < t_idx[:, None]
    log_omb = jnp.where(mask, -jax.nn.softplus(z), 0.0)
    rev = lax.cumsum(log_omb, axis=3, reverse=True)
    log_A = jax.nn.log_sigmoid(z) + (rev - log_omb)
    A = jnp.where(mask, jnp.exp(log_A), 0.0)
    return jnp.einsum("bhts,bhsd->bhtd", A, vp)

def stick_breaking_mixer(h, w_qkv, w_out):
    B, S, _ = h.shape
    qkv = (h @ w_qkv).astype(jnp.float32).reshape(B, S, 3, SB_HEADS, SB_HEAD_DIM)
    qkv = jnp.transpose(qkv, (2, 0, 3, 1, 4))
    q, k, v = qkv[0], qkv[1], qkv[2]
    outs = []
    for start in range(0, S, SB_BLOCK):
        end = start + SB_BLOCK
        outs.append(_stick_breaking_block(q[:, :, start:end], k[:, :, :end], v[:, :, :end], start))
    o = jnp.concatenate(outs, axis=2)
    o = jnp.transpose(o, (0, 2, 1, 3)).reshape(B, S, SB_HEADS * SB_HEAD_DIM).astype(h.dtype)
    return o @ w_out

def swiglu(h, w1, w3, w2):
    return (jax.nn.silu(h @ w1) * (h @ w3)) @ w2

def setup_inputs(seed: int = 0) -> dict:
    key = jax.random.key(seed)
    ks = jax.random.split(key, 24)
    f32 = jnp.float32
    ne, no = (DEPTH + 1) // 2, DEPTH // 2

    def nrm(k, shape, scale):
        return jax.random.normal(k, shape, f32) * scale

    u = jax.random.uniform(ks[13], (ne, LRU_WIDTH), f32, 0.9, 0.999)
    mlstm_gate_b = jnp.stack([nrm(ks[14], (ne, MLSTM_HEADS), 0.1),
                              jax.random.uniform(ks[15], (ne, MLSTM_HEADS), f32, 3.0, 6.0)], axis=1)
    return {
        "x": nrm(ks[0], (BATCH, SEQ, D_MODEL), 1.0),
        "c": nrm(ks[1], (BATCH, D_MODEL), 1.0),
        "ada_w": nrm(ks[2], (DEPTH, 2, D_MODEL, 3 * D_MODEL), 0.5 * D_MODEL ** -0.5),
        "ada_b": nrm(ks[3], (DEPTH, 2, 3 * D_MODEL), 0.02),
        "norm_g": 1.0 + nrm(ks[4], (DEPTH, 2, D_MODEL), 0.02),
        "final_g": 1.0 + nrm(ks[5], (D_MODEL,), 0.02),
        "ffn_w1": nrm(ks[6], (DEPTH, D_MODEL, FFN_HIDDEN), D_MODEL ** -0.5),
        "ffn_w3": nrm(ks[7], (DEPTH, D_MODEL, FFN_HIDDEN), D_MODEL ** -0.5),
        "ffn_w2": nrm(ks[8], (DEPTH, FFN_HIDDEN, D_MODEL), FFN_HIDDEN ** -0.5),
        "ab_w_in": nrm(ks[9], (ne, D_MODEL, AB_IN), D_MODEL ** -0.5),
        "ab_w_out": nrm(ks[10], (ne, MIX_WIDTH, D_MODEL), MIX_WIDTH ** -0.5),
        "lru_conv_w": nrm(ks[11], (ne, CONV_W, LRU_WIDTH), CONV_W ** -0.5),
        "lru_conv_b": nrm(ks[12], (ne, LRU_WIDTH), 0.02),
        "lru_gate_w": nrm(ks[16], (ne, 2, LRU_BLOCKS, LRU_BLOCK_W, LRU_BLOCK_W), LRU_BLOCK_W ** -0.5),
        "lru_gate_b": nrm(ks[17], (ne, 2, LRU_WIDTH), 0.02),
        "lru_lambda": jnp.log(u) - jnp.log1p(-u),
        "mlstm_gate_b": mlstm_gate_b,
        "mlstm_norm_g": 1.0 + nrm(ks[18], (ne, MLSTM_WIDTH), 0.02),
        "sb_w_qkv": nrm(ks[19], (no, D_MODEL, 3 * SB_HEADS * SB_HEAD_DIM), D_MODEL ** -0.5),
        "sb_w_out": nrm(ks[20], (no, SB_HEADS * SB_HEAD_DIM, D_MODEL), (SB_HEADS * SB_HEAD_DIM) ** -0.5),
    }

def reference(x, c, ada_w, ada_b, norm_g, final_g, ffn_w1, ffn_w3, ffn_w2,
              ab_w_in, ab_w_out, lru_conv_w, lru_conv_b, lru_gate_w, lru_gate_b, lru_lambda,
              mlstm_gate_b, mlstm_norm_g, sb_w_qkv, sb_w_out):
    c_act = jax.nn.silu(c)
    for layer in range(DEPTH):
        j = layer // 2
        shift, scale, gate = jnp.split(c_act @ ada_w[layer, 0] + ada_b[layer, 0], 3, axis=-1)
        hn = rmsnorm(x, norm_g[layer, 0]) * (1.0 + scale[:, None, :]) + shift[:, None, :]
        if layer % 2 == 0:
            y = rglru_mlstm_mixer(hn, ab_w_in[j], ab_w_out[j], lru_conv_w[j], lru_conv_b[j],
                                  lru_gate_w[j], lru_gate_b[j], lru_lambda[j],
                                  mlstm_gate_b[j], mlstm_norm_g[j])
        else:
            y = stick_breaking_mixer(hn, sb_w_qkv[j], sb_w_out[j])
        x = x + gate[:, None, :] * y
        shift, scale, gate = jnp.split(c_act @ ada_w[layer, 1] + ada_b[layer, 1], 3, axis=-1)
        hn = rmsnorm(x, norm_g[layer, 1]) * (1.0 + scale[:, None, :]) + shift[:, None, :]
        x = x + gate[:, None, :] * swiglu(hn, ffn_w1[layer], ffn_w3[layer], ffn_w2[layer])
    return rmsnorm(x, final_g)


_drawn_inputs = setup_inputs


def setup_inputs(seed=0):
    import zlib

    import numpy as np

    out = dict(_drawn_inputs(seed))
    spreads = {}
    factors = {'norm_g': 4.498,
     'final_g': 7.544,
     'lru_conv_b': 8.0,
     'lru_gate_b': 8.0,
     'mlstm_norm_g': 27.36}
    for name, (base, spread) in spreads.items():
        noise = np.random.default_rng([zlib.crc32(name.encode()), seed]).standard_normal(out[name].shape)
        drawn = base * np.exp(spread * noise) if base else spread * noise
        out[name] = __import__('jax').numpy.asarray(drawn.astype(out[name].dtype))
    for name, factor in factors.items():
        out[name] = (out[name] * factor).astype(out[name].dtype)
    return out
```

```python
from contextlib import ExitStack

import concourse.bass as bass
from concourse import mybir

ALU = mybir.AluOpType
ACT = mybir.ActivationFunctionType
AX = mybir.AxisListType
F32 = mybir.dt.float32
F32R = mybir.dt.float32r

P = 128
T = 256
D = 2048
KT = D // P
FFN = 5632
FT = FFN // P
EPS = 1e-6
HM = 4
DK = 128
DV = 256
DH = 128
LT = 8
LRU_C = 8.0
GROUPS = [16, 16, 12]
CH = 4
HALF = D // 2
HK = KT // 2
NEVER = -1e30
CREDIT = 4
EARLY = 2 * KT

UP = [2 * n // CH for n in GROUPS]
DOWN = KT // CH
FFN_BODIES = sum(UP) + DOWN * len(GROUPS)
IN0 = 0
OUT0 = IN0 + 10
FFN0 = OUT0 + DOWN
IN1 = FFN0 + FFN_BODIES
OUT1 = IN1 + 12
FFN1 = OUT1 + DOWN
BODIES = FFN1 + FFN_BODIES
LAST_UPDATE = [None, OUT0, FFN0 + FFN_BODIES - DOWN, OUT1, BODIES - DOWN]
UPDATES = {"out0": 0, "down0": KT, "out1": KT * 4, "down1": KT * 5}


def run_stream(eng, body, between):
    def bodies(first, count, kind, pair=0, units=0, q=0, i0=0):
        with eng.Fori(0, count) as i:
            body(i + first, kind, q, i + i0, i * (units // 2) + pair, units)

    def ffn(first, layer):
        up, down = f"up{layer}", f"down{layer}"

        def group(q, pair, units):
            b = q * (UP[0] + DOWN) + first
            with eng.Fori(0, UP[0]) as i:
                body(b + i, up, q, i, pair + i, units)
            units = 0 if layer else units
            with eng.Fori(0, DOWN) as i:
                body(b + UP[0] + i, down, q, i, pair + UP[0] + i, units)

        b = first + 2 * (UP[0] + DOWN)
        if layer:
            group(0, 88, 2)
            group(1, 0, 0)
            bodies(b, UP[2], up, q=2)
            bodies(b + UP[2], DOWN - 1, down + "short", q=2)
            body(b + UP[2] + DOWN - 1, down + "short", 2, DOWN - 1, 0, -1)
        else:
            with eng.Fori(0, 2) as q:
                group(q, q * (UP[0] + DOWN) + 40, 2)
            bodies(b, UP[2], up, 64, 2, q=2)
            bodies(b + UP[2], 2, down + "short", 70, 2, q=2)
            bodies(b + UP[2] + 2, DOWN - 2, down + "short", q=2, i0=2)

    between("start", None)
    between("prologue", None)
    between("norm", 0)
    bodies(IN0, 2, "x_branch", 16, 4)
    between("lru", None)
    bodies(IN0 + 2, 2, "y_branch", 20, 4)
    between("gelu", None)
    bodies(IN0 + 4, 2, "qk", 24, 4)
    bodies(IN0 + 6, 2, "v", 28, 4)
    between("gates", None)
    bodies(IN0 + 8, 2, "o", 32, 4)
    between("mlstm", None)
    bodies(OUT0, DOWN, "out0", 36, 2)
    between("norm", 1)
    ffn(FFN0, 0)
    between("norm", 2)
    with eng.Fori(0, 4) as g:
        b = g * 3 + IN1
        for j, kind in enumerate(("q", "k", "vs")):
            body(b + j, kind, 0, 0, g * 3 + (72 + j), 2)
        between("attend", g)
    bodies(OUT1, DOWN, "out1", 84, 2)
    between("norm", 3)
    ffn(FFN1, 1)
    between("norm", 4)


def split_lead(n, s):
    return n + (s + 2) // CH, (s + 2) % CH


def bass_trunk(nc, xT, c_row, wts, ada, ada_b, norm_g, wgate, conv, lru_w, lru_b, lam, gate_b, mnorm_g, out):
    with ExitStack() as ctx:
        def sb(name, shape, dt=F32):
            return ctx.enter_context(nc.sbuf_tensor(name, shape, dt))

        def sem(name):
            return ctx.enter_context(nc.semaphore(name))

        ps = ctx.enter_context(nc.psum_tensor("ps", [P, 8, 512], F32))

        x = sb("x", [P, KT, T])
        hn = sb("hn", [P, KT, 2, T], F32R)
        mid = sb("mid", [P, KT, 2, T], F32R)
        raw = sb("raw", [P, CH, D])
        whigh = sb("whigh", [P, 4, HALF], F32R)
        wlow = sb("wlow", [P, 4, HALF], F32R)
        adaw = sb("adaw", [P, 2, D])
        cact = sb("cact", [P, D])
        work = sb("work", [P, 34, T])
        mod = sb("mod", [P, 12 * KT])
        dots = sb("dots", [P, 4])
        gains = sb("gains", [P, 5, KT])
        slope = sb("slope", [P, KT])
        rstd = sb("rstd", [P, T])
        ones = sb("ones", [P, P])
        minus = sb("minus", [P, P])
        ident = sb("ident", [P, P])
        tri = sb("tri", [P, P])
        shut = sb("shut", [P, 2, P])
        epsb = sb("epsb", [P, 1])
        convw = sb("convw", [P, LT, 5])
        lrub = sb("lrub", [P, 2, LT])
        lamb = sb("lamb", [P, LT])
        lamt = sb("lamt", [P, 4, LT])
        lruc = sb("lruc", [P, 2, LT])
        mng = sb("mng", [P, 8])
        gb = sb("gb", [HM, 2])
        gtok = sb("gtok", [P, 2, 8])
        gcol = sb("gcol", [P, 2, HM])

        weight_loaded = [sem(f"weight_loaded{s}") for s in range(CH)]
        ada_loaded = [sem(f"ada_loaded{s}") for s in range(2)]
        names = """c_loaded x_loaded small_loaded lru_w_loaded stored
            high_ready low_ready halves_multiplied chunks_evicted half_added
            unit_done mod_added c_ready consts_ready
            square_step variance_ready std_ready rstd_ready slope_ready scaled_ready
            hn_high_ready hn_ready final_ready
            silu_ready hidden_product hidden_high hidden_ready
            gate_w_high gate_w_ready lam_abs lam_exp lam_ready
            conv_ready lru_gates_ready lru_a_ready lru_in_gated lru_root_in lru_roots lru_state gelu_ready
            mixer_low
            gates_summed gate_tokens gate_rows v_turned v_token_a v_token_b forget_abs forget_exp forget_log
            decay_rows gate_cols gate_cols_read m_scores_raw m_weights m_floor m_scored m_products m_den_abs m_normed
            m_squared m_meansq m_roots m_rstd o_ready m_out m_high
            s_v_turned s_v_token s_q_scaled s_scores s_abs s_exp1 s_log s_softplus s_masked s_logits s_probs
            s_out s_high s_low dve_chain act_chain pool_chain""".split()
        S = {n: sem(n) for n in names}

        XA, XC, GW, W8 = (work[:, i:i + 8, :] for i in (0, 8, 16, 24))

        def flat(ap):
            return ap.rearrange("p a t -> p (a t)")

        vtok = [flat(work[:, 16 + 4 * j:20 + 4 * j, :]) for j in range(2)]

        def m_weight(h):
            return flat(work[:, 24:27, :])[:, (h % 2) * (T + P):(h % 2 + 1) * (T + P)]

        def m_score(h):
            return flat(work[:, 27 + 2 * (h % 2):29 + 2 * (h % 2), :])

        def m_floor_row(h):
            return rstd[:, :] if h % 2 else work[:, 31, :]

        s_vtok = flat(work[:, 12:16, :]).rearrange("p (j n) -> p j n", j=2)

        def s_soft(w):
            return flat(work[:, 16 + 3 * w:19 + 3 * w, :]).rearrange("p (h n) -> p h n", h=2)

        def s_tmp(w):
            return flat(work[:, 22 + 3 * w:25 + 3 * w, :]).rearrange("p (h n) -> p h n", h=2)

        def row(i):
            return work[0:HM, 26 + i, :]

        squares_sum = work[:, 31, :]
        square = work[:, 32, :]
        wg = mid[:, KT - 1, 0, :].rearrange("p (k h g) -> p k h g", k=KT, h=2)
        wg_raw = work[:, 30, 0:8 * KT].rearrange("p (k g) -> p k g", g=8)

        def mod_vec(i, m=slice(0, KT)):
            return mod[:, i * KT:i * KT + KT][:, m]

        def units_count(v):
            return (v + 1) * KT

        def unit_place(u):
            slot = u % 4
            if slot < 2:
                return adaw[:, slot, :], ada_loaded[slot], u // 4
            return raw[:, slot, :], weight_loaded[slot], u // 4

        EARLY_LOADS = EARLY // 4

        def weight_count(n, s):
            return (n + (EARLY_LOADS if s >= 2 else 0)) * 16 + 16

        block = ctx.enter_context(nc.Block())

        @block.sync
        def _(sp):
            sp.dma_start(cact[:, :], c_row.to_broadcast([P, D])).then_inc(S["c_loaded"], 16)

            def body(n, kind, q, i, pair, units):
                for s in range(CH):
                    if units >= 0:
                        sp.wait_ge(S["low_ready"], n * 8 + 2 * s + 2)
                        sp.dma_start(raw[:, s, :], wts[bass.ds(n * CH + s + CH, 1), :, :].rearrange("a p n -> p (a n)"))\
                          .then_inc(weight_loaded[s], 16)
                    for u in range(s * units // CH, (s + 1) * units // CH):
                        sp.wait_ge(S["unit_done"], pair * 2 + u + 1)
                        sp.dma_start(adaw[:, u % 2, :], ada[bass.ds(pair * 2 + u, 1), :, :].rearrange("a p n -> p (a n)"))\
                          .then_inc(ada_loaded[u % 2], 16)

            def between(name, c):
                if name == "prologue":
                    for u in range(EARLY):
                        place, loaded, before = unit_place(u)
                        if before:
                            sp.wait_ge(S["unit_done"], u - 4 + 3)
                        sp.dma_start(place, ada[u, :, :]).then_inc(loaded, 16)
                        if u == 3:
                            for s in range(2):
                                sp.dma_start(raw[:, s, :], wts[s, :, :]).then_inc(weight_loaded[s], 16)
                        if u == 15:
                            sp.dma_start(x[:, :, :], xT).then_inc(S["x_loaded"], 16)
                    for s in range(2, CH):
                        sp.wait_ge(S["unit_done"], EARLY - CH + s + 3)
                        sp.dma_start(raw[:, s, :], wts[s, :, :]).then_inc(weight_loaded[s], 16)
                if name == "norm" and c == 4:
                    for j in range(4):
                        sp.wait_ge(S["final_ready"], 4 * j + 4)
                        sp.dma_start(out[:, 4 * j:4 * j + 4, :], x[:, 4 * j:4 * j + 4, :]).then_inc(S["stored"], 16)
                    sp.wait_ge(S["stored"], 64)

            run_stream(sp, body, between)

        @block.gpsimd
        def _(pool):
            pool.memset(ones[:, :], 1.0).then_inc(S["pool_chain"], 1)
            pool.memset(minus[:, :], -1.0).then_inc(S["pool_chain"], 1)
            pool.memset(epsb[:, :], EPS).then_inc(S["consts_ready"], 1)
            pool.memset(shut[:, :, :], NEVER).then_inc(S["pool_chain"], 1)
            pool.wait_ge(S["pool_chain"], 3)
            pool.affine_select(out=ident[:, :], in_=ones[:, :], compare_op=ALU.is_equal, fill=0.0, base=0,
                               pattern=[[-1, P]], channel_multiplier=1).then_inc(S["consts_ready"], 1)
            pool.affine_select(out=tri[:, :], in_=minus[:, :], compare_op=ALU.is_ge, fill=0.0, base=0,
                               pattern=[[-1, P]], channel_multiplier=1).then_inc(S["consts_ready"], 1)
            for j, compare in enumerate((ALU.is_gt, ALU.is_ge)):
                pool.affine_select(out=shut[:, j, :], in_=shut[:, j, :], compare_op=compare, fill=0.0, base=0,
                                   pattern=[[-1, P]], channel_multiplier=1).then_inc(S["consts_ready"], 1)

            def squares(norm):
                if norm:
                    pool.wait_ge(S["variance_ready"], norm)
                    pool.wait_ge(S["chunks_evicted"], LAST_UPDATE[norm] * CH + 1 + CREDIT)
                else:
                    pool.wait_ge(S["x_loaded"], 16)
                pool.memset(squares_sum, 0.0).then_inc(S["square_step"], 1)
                with pool.Fori(0, KT) as m:
                    xm = x[:, bass.ds(m, 1), :].rearrange("p a t -> p (a t)")
                    if norm:
                        pool.wait_ge(S["chunks_evicted"], m + LAST_UPDATE[norm] * CH + 1 + CREDIT)
                    pool.wait_ge(S["square_step"], m * 2 + 33 * norm + 1)
                    pool.tensor_tensor(square, xm, xm, ALU.mult).then_inc(S["square_step"], 1)
                    pool.wait_ge(S["square_step"], m * 2 + 33 * norm + 2)
                    pool.tensor_tensor(squares_sum, squares_sum, square, ALU.add).then_inc(S["square_step"], 1)

            def between(name, c):
                if name == "norm":
                    squares(c)
                elif name == "attend":
                    for w in range(2):
                        pool.wait_ge(S["s_softplus"], c * 2 + w + 1)
                        for h in range(2):
                            for block in (slice(0, P), slice(T, T + P)):
                                m = s_soft(w)[:, h, block]
                                pool.affine_select(out=m, in_=m, compare_op=ALU.is_gt, fill=0.0, base=0,
                                                   pattern=[[1, P]], channel_multiplier=-1).then_inc(S["s_masked"], 1)

            between("norm", 0)
            between("norm", 1)
            between("norm", 2)
            for g in range(4):
                between("attend", g)
            between("norm", 3)
            between("norm", 4)

        @block.scalar
        def _(act):
            def split(n, s):
                act.wait_ge(weight_loaded[s], weight_count(n, s))
                for h in range(2):
                    act.wait_ge(S["halves_multiplied"], n * 8 + 2 * s + h + 1)
                    act.activation(whigh[:, (2 * s + h) % 4, :], raw[:, s, h * HALF:(h + 1) * HALF], ACT.Copy)\
                       .then_inc(S["high_ready"], 1)

            def body(n, kind, q, i, pair, units):
                for s in range(CH):
                    if units >= 0 or s < 2:
                        split(*split_lead(n, s))
                    if kind[:2] == "up" and s % 2:
                        act.wait_ge(S["chunks_evicted"], n * CH + s + CREDIT)
                        act.activation(work[:, 2 + s // 2, :], work[:, s // 2, :], ACT.Silu).then_inc(S["silu_ready"], 1)

            def norm(i):
                act.wait_ge(S["variance_ready"], i + 1)
                act.wait_ge(S["consts_ready"], 5)
                if i:
                    act.wait_ge(S["hn_ready"], KT * i)
                act.activation(rstd[:, :], ps[:, 7, 0:T], ACT.Sqrt, scale=1.0 / D, bias=epsb[:, 0:1]).then_inc(S["std_ready"], 1)
                if i < 4:
                    for k in range(KT):
                        act.wait_ge(S["scaled_ready"], KT * i + k + 1)
                        act.activation(hn[:, k, 0, :], work[:, k, :], ACT.Identity, bias=mod_vec(3 * i)[:, k:k + 1])\
                           .then_inc(S["hn_high_ready"], 1)

            def between(name, c):
                if name == "start":
                    for k, (dst, src) in enumerate(((gains[:, :, :], norm_g), (mod[:, :], ada_b), (wg_raw[:, :, :], wgate),
                                                    (convw[:, :, :], conv), (lrub[:, :, :], lru_b), (lamb[:, :], lam),
                                                    (gb[:, :], gate_b), (mng[:, :], mnorm_g))):
                        act.dma_start(dst, src).then_inc(S["small_loaded"], 16)
                    act.dma_start(flat(GW), lru_w).then_inc(S["lru_w_loaded"], 16)
                    act.wait_ge(S["c_loaded"], 16)
                    act.activation(cact[:, :], cact[:, :], ACT.Silu).then_inc(S["c_ready"], 1)
                    act.wait_ge(S["small_loaded"], 16 * 8)
                    act.activation(wg[:, :, 0, :], wg_raw[:, :, :], ACT.Copy).then_inc(S["gate_w_high"], 1)
                    act.wait_ge(S["lam_abs"], 1)
                    act.activation(lamt[:, 1, :], lamt[:, 0, :], ACT.Exp, scale=-1.0).then_inc(S["lam_exp"], 1)
                elif name == "norm":
                    norm(c)
                elif name == "prologue":
                    split(0, 0)
                    split(0, 1)
                elif name == "lru":
                    act.wait_ge(S["lam_ready"], 1)
                    for n in range(LT):
                        bank = ps[:, 4 + n % 2, :]
                        act.wait_ge(S["lru_gates_ready"], n + 1)
                        act.activation(W8[:, n, :], bank[:, 0:T], ACT.Tanh, scale=0.5,
                                       bias=lrub[:, 0, n:n + 1]).then_inc(S["act_chain"], 1)
                        act.activation(bank[:, T:2 * T], bank[:, T:2 * T], ACT.Tanh, scale=0.5,
                                       bias=lrub[:, 1, n:n + 1])
                        act.wait_ge(S["act_chain"], 2 * n + 1)
                        act.activation(XA[:, n, :], W8[:, n, :], ACT.Exp, scale=lruc[:, 0, n:n + 1],
                                       bias=lruc[:, 0, n:n + 1]).then_inc(S["act_chain"], 1)
                        act.wait_ge(S["act_chain"], 2 * n + 2)
                        act.activation(W8[:, n, :], W8[:, n, :], ACT.Tanh, scale=lruc[:, 1, n:n + 1],
                                       bias=lruc[:, 1, n:n + 1]).then_inc(S["lru_a_ready"], 1)
                    act.wait_ge(S["lru_root_in"], LT)
                    act.activation(flat(W8), flat(W8), ACT.Sqrt).then_inc(S["lru_roots"], 1)
                elif name == "gelu":
                    act.wait_ge(S["chunks_evicted"], (IN0 + 4) * CH + CREDIT)
                    act.activation(flat(XC), flat(XC), ACT.Gelu_apprx_tanh).then_inc(S["gelu_ready"], 1)
                elif name == "gates":
                    act.wait_ge(S["v_turned"], 1)
                    act.activation(vtok[0], ps[:, 0:2, :], ACT.Copy).then_inc(S["v_token_a"], 1)
                    act.wait_ge(S["forget_abs"], 1)
                    act.activation(row(2), row(1), ACT.Exp, scale=-1.0).then_inc(S["forget_exp"], 1)
                    act.wait_ge(S["forget_exp"], 1)
                    act.activation(row(2), row(2), ACT.Ln, bias=ones[0:HM, 0:1]).then_inc(S["forget_log"], 1)
                elif name == "mlstm":
                    def squared(h):
                        den = ps[:, 2, (h % 2) * T:(h % 2) * T + T]
                        act.wait_ge(S["m_products"], h + 1)
                        act.activation(den, den, ACT.Abs).then_inc(S["m_den_abs"], 1)
                        act.wait_ge(S["m_normed"], h + 1)
                        act.activation(m_score(h), work[:, h:h + 5:4, :], ACT.Square).then_inc(S["m_squared"], 1)

                    for h in range(HM):
                        bank = ps[:, 4 + h % 2, :]
                        act.wait_ge(S["m_scores_raw"], h + 1)
                        act.wait_ge(S["gate_cols_read"], 1)
                        if h >= 2:
                            act.wait_ge(S["m_scored"], h - 1)
                            act.wait_ge(S["m_normed"], h - 1)
                        act.activation(m_weight(h)[:, 0:T], bank[:, 0:T], ACT.Exp, bias=gcol[:, 0, h:h + 1])
                        act.activation(m_weight(h)[:, T:T + P], bank[:, T:T + P], ACT.Exp, bias=gcol[:, 1, h:h + 1])\
                           .then_inc(S["m_weights"], 1)
                        act.activation(m_floor_row(h), ps[:, 3 + 4 * (h // 2), (h % 2) * T:(h % 2) * T + T], ACT.Exp).then_inc(S["m_floor"], 1)
                        if h:
                            squared(h - 1)
                    squared(HM - 1)
                    act.activation(flat(XC), flat(XC), ACT.Tanh, scale=0.5).then_inc(S["o_ready"], 1)
                    act.wait_ge(S["m_meansq"], HM)
                    act.activation(work[:, 24:28, :], ps[:, 3:8:4, :], ACT.Sqrt, scale=1.0 / DV, bias=epsb[:, 0:1])\
                       .then_inc(S["m_roots"], 1)
                    act.wait_ge(S["m_out"], 8)
                    act.activation(mid[:, 8:16, 0, :], XC[:, :, :], ACT.Copy).then_inc(S["m_high"], 1)
                elif name == "attend":
                    g = c
                    act.wait_ge(S["s_v_turned"], g + 1)
                    act.activation(s_vtok, ps[:, 0:2, :], ACT.Copy).then_inc(S["s_v_token"], 1)
                    for w in range(2):
                        act.wait_ge(S["s_scores"], g * 2 + w + 1)
                        act.activation(s_tmp(w), ps[:, 4 + 2 * w:6 + 2 * w, 0:T + P], ACT.Abs).then_inc(S["s_abs"], 1)
                        act.wait_ge(S["s_abs"], g * 2 + w + 1)
                        act.activation(s_tmp(w), s_tmp(w), ACT.Exp, scale=-1.0).then_inc(S["s_exp1"], 1)
                        act.wait_ge(S["s_exp1"], g * 2 + w + 1)
                        act.activation(s_tmp(w), s_tmp(w), ACT.Ln, bias=ones[:, 0:1]).then_inc(S["s_log"], 1)
                    for w in range(2):
                        act.wait_ge(S["s_logits"], g * 2 + w + 1)
                        act.activation(s_tmp(w), ps[:, 4 + 2 * w:6 + 2 * w, 0:T + P], ACT.Exp).then_inc(S["s_probs"], 1)
                    for w in range(2):
                        act.wait_ge(S["s_out"], g * 2 + w + 1)
                        act.activation(mid[:, bass.ds(g * 4 + 2 * w, 2), 0, :], ps[:, 2 + w, :].rearrange("p (h t) -> p h t", h=2),
                                       ACT.Copy).then_inc(S["s_high"], 1)

            run_stream(act, body, between)

        @block.vector
        def _(dve):
            links = [0]

            def link(ins):
                links[0] += 1
                ins.then_inc(S["dve_chain"], 1)
                dve.wait_ge(S["dve_chain"], links[0])

            def split(n, s):
                for h in range(2):
                    dve.wait_ge(S["high_ready"], n * 8 + 2 * s + h + 1)
                    half = (2 * s + h) % 4
                    dve.tensor_tensor(wlow[:, half, :], raw[:, s, h * HALF:(h + 1) * HALF], whigh[:, half, :].bitcast(F32),
                                      ALU.subtract).then_inc(S["low_ready"], 1)

            def add_unit(place, u, first):
                if u == 0 and first is not None:
                    dve.wait_ge(S["mod_added"], first)
                dve.tensor_tensor_reduce(out=place, in0=place, in1=cact[:, :], scale=1.0, scalar=0.0, op0=ALU.mult,
                                         op1=ALU.add, accum_out=dots[:, u:u + 1]).then_inc(S["unit_done"], 1)

            def add_to_mod(first, units):
                dve.wait_ge(S["unit_done"], first + units + 2)
                columns = mod[:, bass.ds(first, units)]
                dve.tensor_tensor(columns, columns, dots[:, 0:units], ALU.add).then_inc(S["mod_added"], units)

            def units_of(pair, units, s):
                for u in range(s * units // CH, (s + 1) * units // CH):
                    dve.wait_ge(ada_loaded[u % 2], (pair + (u // 2 - EARLY // 2 + EARLY_LOADS)) * 16 + 16)
                    add_unit(adaw[:, u % 2, :], u, pair * 2)

            def halves_sum(s):
                return ps[:, s, :].rearrange("p (h t) -> p t h", h=2)

            def sum_halves(dst, s):
                dve.tensor_reduce(dst, halves_sum(s), AX.X, ALU.add).then_inc(S["chunks_evicted"], 1)

            def update_x(n, s, kind, q, i):
                norm = {"out0": 0, "down0": 1, "out1": 2, "down1": 3}[kind]
                count = q * KT + i * CH + UPDATES[kind] + s
                m = bass.ds(i * CH + s, 1)
                gate = mod[:, bass.ds(i * CH + (s + (3 * norm + 2) * KT), 1)]
                dve.wait_ge(S["mod_added"], units_count(3 * norm + 2))
                tmp = work[:, 8 + s, :]
                xm = x[:, m, :].rearrange("p a t -> p (a t)")
                dve.scalar_tensor_tensor(tmp, ps[:, s, 0:T], gate, xm, ALU.mult, ALU.add).then_inc(S["half_added"], 1)
                dve.wait_ge(S["half_added"], count + 1)
                dve.scalar_tensor_tensor(xm, ps[:, s, T:2 * T], gate, tmp, ALU.mult, ALU.add).then_inc(S["chunks_evicted"], 1)

            def body(n, kind, q, i, pair, units):
                for s in range(CH):
                    if units >= 0 or s < 2:
                        split(*split_lead(n, s))
                    dve.wait_ge(S["halves_multiplied"], n * 8 + 2 * s + 2 + CREDIT)
                    base = {"x_branch": 0, "y_branch": 8, "qk": 0, "v": 8, "o": 8, "q": 0, "k": 4, "vs": 8}
                    if kind in base:
                        sum_halves(work[:, bass.ds(i * CH + base[kind] + s, 1), :].rearrange("p a t -> p (a t)"), s)
                    elif kind[:2] == "up":
                        j = s // 2
                        if s % 2 == 0:
                            sum_halves(work[:, j, :], s)
                            units_of(pair, units, s)
                        else:
                            layer = int(kind[2])
                            tile = i * 2 + j
                            count = q * GROUPS[0] + i * 2 + (layer * FT + j)
                            sum_halves(work[:, 4 + j, :], s)
                            units_of(pair, units, s)
                            dve.wait_ge(S["silu_ready"], count + 1)
                            dve.wait_ge(S["chunks_evicted"], n * CH + s + 1 + CREDIT)
                            dve.tensor_tensor(work[:, 6 + j, :], work[:, 2 + j, :], work[:, 4 + j, :], ALU.mult)\
                               .then_inc(S["hidden_product"], 1)
                            dve.wait_ge(S["hidden_product"], count + 1)
                            high = mid[:, bass.ds(tile, 1), 0, :].rearrange("p a t -> p (a t)")
                            low = mid[:, bass.ds(tile, 1), 1, :].rearrange("p a t -> p (a t)")
                            dve.tensor_copy(high, work[:, 6 + j, :]).then_inc(S["hidden_high"], 1)
                            dve.wait_ge(S["hidden_high"], count + 1)
                            dve.tensor_tensor(low, work[:, 6 + j, :], high.bitcast(F32), ALU.subtract).then_inc(S["hidden_ready"], 1)
                    else:
                        update_x(n, s, kind.replace("short", ""), q, i)
                    if kind[:2] != "up":
                        units_of(pair, units, s)
                if units > 0:
                    add_to_mod(pair * 2, units)

            def norm(i):
                if i < 4:
                    dve.wait_ge(S["mod_added"], units_count(3 * i + 1))
                    dve.scalar_tensor_tensor(slope[:, :], mod_vec(3 * i + 1), 1.0, gains[:, i, :], ALU.add, ALU.mult)\
                       .then_inc(S["slope_ready"], 1)
                dve.wait_ge(S["std_ready"], i + 1)
                dve.reciprocal(rstd[:, :], rstd[:, :]).then_inc(S["rstd_ready"], 1)
                dve.wait_ge(S["rstd_ready"], i + 1)
                if i == 4:
                    for k in range(KT):
                        dve.scalar_tensor_tensor(x[:, k, :], x[:, k, :], gains[:, 4, k:k + 1], rstd[:, :],
                                                 ALU.mult, ALU.mult).then_inc(S["final_ready"], 1)
                    return
                dve.wait_ge(S["slope_ready"], i + 1)

                def low(k):
                    dve.wait_ge(S["hn_high_ready"], KT * i + k + 1)
                    dve.scalar_tensor_tensor(hn[:, k, 1, :], work[:, k, :], mod_vec(3 * i)[:, k:k + 1],
                                             hn[:, k, 0, :].bitcast(F32), ALU.add, ALU.subtract).then_inc(S["hn_ready"], 1)

                for k in range(KT):
                    dve.scalar_tensor_tensor(work[:, k, :], x[:, k, :], slope[:, k:k + 1], rstd[:, :], ALU.mult, ALU.mult)\
                       .then_inc(S["scaled_ready"], 1)
                    if k:
                        low(k - 1)
                low(KT - 1)

            def between(name, c):
                if name == "start":
                    dve.sem_inc(S["unit_done"], 2)
                    dve.sem_inc(S["chunks_evicted"], CREDIT)
                    dve.wait_ge(S["small_loaded"], 16 * 8)
                    dve.scalar_tensor_tensor(lamt[:, 0, :], lamb[:, :], -1.0, lamb[:, :], ALU.mult, ALU.max).then_inc(S["lam_abs"], 1)
                    dve.wait_ge(S["gate_w_high"], 1)
                    dve.tensor_tensor(wg[:, :, 1, :], wg_raw[:, :, :], wg[:, :, 0, :].bitcast(F32), ALU.subtract)\
                       .then_inc(S["gate_w_ready"], 1)
                    dve.tensor_scalar(lrub[:, :, :], lrub[:, :, :], 0.5, None, ALU.mult)
                    dve.tensor_scalar(mng[:, :], mng[:, :], 0.5, None, ALU.mult)
                    dve.wait_ge(S["lam_exp"], 1)
                    e, t, s, s2 = lamt[:, 1, :], lamt[:, 2, :], lamt[:, 0, :], lamt[:, 3, :]
                    link(dve.tensor_scalar(t, e, 2.0, None, ALU.add))
                    link(dve.reciprocal(t, t))
                    link(dve.tensor_tensor(s, e, t, ALU.mult))
                    link(dve.tensor_tensor(s2, s, s, ALU.mult))
                    link(dve.tensor_scalar(t, s2, 1.0 / 15, None, ALU.mult))
                    for k in (13, 11, 9, 7, 5, 3):
                        link(dve.scalar_tensor_tensor(t, t, 1.0 / k, s2, ALU.add, ALU.mult))
                    link(dve.scalar_tensor_tensor(t, t, 1.0, s, ALU.add, ALU.mult))
                    link(dve.tensor_scalar(s2, lamb[:, :], 0.0, None, ALU.min))
                    link(dve.scalar_tensor_tensor(t, t, -2.0, s2, ALU.mult, ALU.add))
                    dve.tensor_scalar(lruc[:, 0, :], t, LRU_C / 2, None, ALU.mult)
                    dve.tensor_scalar(lruc[:, 1, :], t, -LRU_C / 2, None, ALU.mult).then_inc(S["lam_ready"], 1)
                    dve.wait_ge(S["c_ready"], 1)
                elif name == "prologue":
                    for u in range(EARLY):
                        place, loaded, before = unit_place(u)
                        dve.wait_ge(loaded, before * 16 + 16)
                        add_unit(place, u % 4, u or None)
                        if u % 4 == 3:
                            add_to_mod(u - 3, 4)
                        if u == 7:
                            split(0, 0)
                            split(0, 1)
                elif name == "norm":
                    norm(c)
                elif name == "lru":
                    dve.wait_ge(S["chunks_evicted"], (IN0 + 2) * CH + CREDIT)
                    for n in range(LT):
                        link(dve.tensor_scalar(XC[:, n, :], XA[:, n, :], convw[:, n, 3:4], convw[:, n, 4:5], ALU.mult, ALU.add))
                        for back in (1, 2, 3):
                            ins = dve.scalar_tensor_tensor(XC[:, n, back:T], XA[:, n, 0:T - back], convw[:, n, 3 - back:4 - back],
                                                           XC[:, n, back:T], ALU.mult, ALU.add)
                            if back < 3:
                                link(ins)
                        ins.then_inc(S["conv_ready"], 1)
                    for n in range(LT):
                        bank = ps[:, 4 + n % 2, :]
                        dve.wait_ge(S["lru_a_ready"], n + 1)
                        dve.wait_ge(S["conv_ready"], LT)
                        dve.scalar_tensor_tensor(XC[:, n, :], bank[:, T:2 * T], 1.0, XC[:, n, :], ALU.add, ALU.mult)\
                           .then_inc(S["lru_in_gated"], 1)
                        link(dve.tensor_tensor(bank[:, 0:T], XA[:, n, :], XA[:, n, :], ALU.mult))
                        dve.scalar_tensor_tensor(W8[:, n, :], bank[:, 0:T], 1.0, W8[:, n, :], ALU.add, ALU.mult)\
                           .then_inc(S["lru_root_in"], 1)
                    dve.wait_ge(S["lru_roots"], 1)
                    dve.wait_ge(S["lru_in_gated"], LT)
                    link(dve.scalar_tensor_tensor(flat(XC), flat(W8), 0.5, flat(XC), ALU.mult, ALU.mult))
                    for n in range(LT):
                        dve.tensor_tensor_scan(W8[:, n, :], XA[:, n, :], XC[:, n, :], 0.0, ALU.mult, ALU.add)\
                           .then_inc(S["lru_state"], 1)
                    dve.wait_ge(S["lru_state"], LT)
                elif name == "gelu":
                    dve.wait_ge(S["gelu_ready"], 1)
                    link(dve.tensor_tensor(flat(W8), flat(W8), flat(XC), ALU.mult))
                    link(dve.tensor_copy(mid[:, 0:8, 0, :], W8[:, :, :]))
                    dve.tensor_tensor(mid[:, 0:8, 1, :], W8[:, :, :], mid[:, 0:8, 0, :].bitcast(F32), ALU.subtract)\
                       .then_inc(S["mixer_low"], 1)
                    dve.wait_ge(S["mixer_low"], 1)
                elif name == "gates":
                    dve.wait_ge(S["gates_summed"], 1)
                    for j in range(2):
                        ins = dve.tensor_reduce(gtok[:, j, :], ps[:, 5, 16 * j:16 * j + 16].rearrange("p (h t) -> p t h", h=2),
                                                AX.X, ALU.add)
                    ins.then_inc(S["gate_tokens"], 1)
                    dve.wait_ge(S["v_turned"], 1)
                    dve.tensor_copy(vtok[1], ps[:, 2:4, :]).then_inc(S["v_token_b"], 1)
                    dve.wait_ge(S["gate_rows"], 1)
                    dve.tensor_scalar(row(3), ps[0:HM, 4, 0:T], gb[:, 0:1], None, ALU.add)
                    dve.memset(row(4), 0.0)
                    link(dve.tensor_scalar(row(0), ps[0:HM, 4, T:2 * T], gb[:, 1:2], None, ALU.add))
                    dve.scalar_tensor_tensor(row(1), row(0), -1.0, row(0), ALU.mult, ALU.max).then_inc(S["forget_abs"], 1)
                    link(dve.tensor_scalar(row(0), row(0), 0.0, None, ALU.min))
                    dve.wait_ge(S["forget_log"], 1)
                    link(dve.tensor_tensor(row(0), row(0), row(2), ALU.subtract))
                    dve.wait_ge(S["consts_ready"], 5)
                    link(dve.tensor_tensor_scan(row(2), row(0), row(4), 0.0, ALU.add, ALU.add))
                    link(dve.tensor_tensor(row(5), row(3), row(2), ALU.subtract))
                    link(dve.tensor_tensor_scan(row(1), row(5), row(5), 0.0, ALU.max, ALU.max))
                    dve.tensor_scalar(row(6), row(1), -1.0, None, ALU.mult)
                    dve.scalar_tensor_tensor(row(7), row(2), -1.0, row(1), ALU.mult, ALU.subtract)\
                       .then_inc(S["decay_rows"], 1)
                    dve.wait_ge(S["gate_cols"], 1)
                    dve.tensor_copy(gcol[:, :, :], ps[:, 6, 0:2 * HM].rearrange("p (a h) -> p a h", a=2)).then_inc(S["gate_cols_read"], 1)
                elif name == "mlstm":
                    def scored(h):
                        dve.wait_ge(S["m_weights"], h + 1)
                        if h >= 2:
                            dve.wait_ge(S["m_meansq"], h - 1)
                        dve.scalar_tensor_tensor(m_score(h)[:, 0:T + P], ps[:, 6, 0:T + P], float(DK) ** -0.5,
                                                 m_weight(h)[:, 0:T + P], ALU.mult, ALU.mult).then_inc(S["m_scored"], 1)

                    def normed(h):
                        f = m_floor_row(h)
                        dve.wait_ge(S["m_den_abs"], h + 1)
                        link(dve.tensor_tensor(f, ps[:, 2, (h % 2) * T:(h % 2) * T + T], f, ALU.max))
                        link(dve.reciprocal(f, f))
                        dve.tensor_tensor(work[:, h:h + 5:4, :], ps[:, h % 2, :].rearrange("p (a t) -> p a t", a=2),
                                          f.rearrange("p (a t) -> p a t", a=1).to_broadcast([P, 2, T]), ALU.mult)\
                           .then_inc(S["m_normed"], 1)

                    scored(0)
                    for h in range(1, HM):
                        scored(h) if h == 1 else None
                        normed(h - 1)
                        if h + 1 < HM:
                            scored(h + 1)
                    normed(HM - 1)
                    dve.wait_ge(S["o_ready"], 1)
                    dve.wait_ge(S["m_normed"], HM)
                    for v in range(2):
                        o = XC[:, v:8:2, :]
                        ins = dve.scalar_tensor_tensor(o, o, 1.0, work[:, 4 * v:4 * v + 4, :], ALU.add, ALU.mult)
                    link(ins)
                    dve.wait_ge(S["m_roots"], 1)
                    link(dve.reciprocal(flat(work[:, 24:28, :]), flat(work[:, 24:28, :])))
                    for j in range(8):
                        dve.scalar_tensor_tensor(XC[:, j, :], XC[:, j, :], mng[:, j:j + 1], work[:, 24 + j // 2, :],
                                                 ALU.mult, ALU.mult).then_inc(S["m_out"], 1)
                    dve.wait_ge(S["m_high"], 1)
                    dve.tensor_tensor(mid[:, 8:16, 1, :], XC[:, :, :], mid[:, 8:16, 0, :].bitcast(F32), ALU.subtract)\
                       .then_inc(S["mixer_low"], 1)
                elif name == "attend":
                    g = c
                    q4 = flat(work[:, 0:4, :])
                    dve.wait_ge(S["chunks_evicted"], (g * 3 + IN1 + 3) * CH + CREDIT)
                    dve.tensor_scalar(q4, q4, float(DH) ** -0.5, None, ALU.mult).then_inc(S["s_q_scaled"], 1)
                    for w in range(2):
                        z = ps[:, 4 + 2 * w:6 + 2 * w, 0:T + P]
                        dve.wait_ge(S["s_log"], g * 2 + w + 1)
                        dve.scalar_tensor_tensor(s_soft(w), z, 0.0, s_tmp(w), ALU.max, ALU.add).then_inc(S["s_softplus"], 1)
                    for w in range(2):
                        dve.wait_ge(S["s_high"], g * 2 + w + 1)
                        m = mid[:, bass.ds(g * 4 + 2 * w, 2), :, :]
                        dve.tensor_tensor(m[:, :, 1, :], ps[:, 2 + w, :].rearrange("p (h t) -> p h t", h=2),
                                          m[:, :, 0, :].bitcast(F32), ALU.subtract).then_inc(S["s_low"], 1)

            run_stream(dve, body, between)

        @block.tensor
        def _(pe):
            def body(n, kind, q, i, pair, units):
                src = mid if kind[:3] in ("out", "dow") else hn
                kts = GROUPS[2] if "short" in kind else KT
                for s in range(CH):
                    pe.wait_ge(S["chunks_evicted"], n * CH + s + 1)
                    for h in range(2):
                        pe.wait_ge(S["low_ready"], n * 8 + 2 * s + h + 1)
                        half = (2 * s + h) % 4
                        for k in range(min(HK, kts - h * HK)):
                            kk = h * HK + k
                            if kind[:4] == "down":
                                if kk >= kts - 4 or kk % 4 == 0:
                                    first = q * GROUPS[0] + int(kind[4]) * FT
                                    pe.wait_ge(S["hidden_ready"], first + (kk + 1 if kk >= kts - 4 else kk + 4))
                            elif kind[:3] != "out" and s == 0:
                                norm = {"up0": 1, "q": 2, "k": 2, "vs": 2, "up1": 3}.get(kind, 0)
                                pe.wait_ge(S["hn_ready"], KT * norm + kk + 1)
                            w = slice(k * P, k * P + P)
                            pe.matmul(ps[:, s, :], whigh[:, half, w], src[:, kk, :, :], start=kk == 0, stop=False,
                                      skip_group_check=True)
                            ins = pe.matmul(ps[:, s, T:2 * T], wlow[:, half, w], src[:, kk, 0, :], start=False,
                                            stop=kk == kts - 1, skip_group_check=True)
                        ins.then_inc(S["halves_multiplied"], 1)

            def between(name, c):
                if name == "start":
                    pe.sem_inc(S["halves_multiplied"], CREDIT)
                elif name == "norm":
                    pe.wait_ge(S["square_step"], 33 * c + 33)
                    pe.matmul(ps[:, 7, 0:T], ones[:, :], squares_sum, start=True, stop=True).then_inc(S["variance_ready"], 1)
                elif name == "lru":
                    pe.wait_ge(S["lru_w_loaded"], 16)
                    gw = flat(GW).rearrange("p (g n e) -> p g n e", g=2, n=LT)
                    for n in range(LT):
                        pe.wait_ge(S["conv_ready"], n + 1)
                        if n >= 2:
                            pe.wait_ge(S["lru_root_in"], n - 1)
                        pe.matmul(ps[:, 4 + n % 2, 0:T], gw[:, 0, n, :], XC[:, n, :], start=True, stop=True)
                        pe.matmul(ps[:, 4 + n % 2, T:2 * T], gw[:, 1, n, :], XC[:, n, :], start=True, stop=True)\
                          .then_inc(S["lru_gates_ready"], 1)
                elif name == "gates":
                    pe.wait_ge(S["gate_w_ready"], 1)
                    pe.wait_ge(S["lru_root_in"], LT)
                    for j in range(2):
                        for k in range(KT):
                            tok = slice(j * P, j * P + P)
                            pe.matmul(ps[:, 5, 16 * j:16 * j + 16], hn[:, k, 0, tok], wg[:, k, :, :], start=k == 0, stop=False,
                                      skip_group_check=True)
                            ins = pe.matmul(ps[:, 5, 16 * j + 8:16 * j + 16], hn[:, k, 1, tok], wg[:, k, 0, :], start=False,
                                            stop=k == KT - 1, skip_group_check=True)
                    ins.then_inc(S["gates_summed"], 1)
                    pe.wait_ge(S["chunks_evicted"], (IN0 + 8) * CH + CREDIT)
                    for j in range(2):
                        for v in range(8):
                            ins = pe.transpose(ps[:, 2 * j + v // 4, (v % 4) * P:(v % 4) * P + P], XC[:, v, j * P:j * P + P], ident[:, :])
                    ins.then_inc(S["v_turned"], 1)
                    pe.wait_ge(S["gate_tokens"], 1)
                    for which in range(2):
                        for j in range(2):
                            ins = pe.matmul(ps[0:HM, 4, which * T + j * P:which * T + j * P + P], gtok[:, j, HM * which:HM * which + HM],
                                            ident[:, :], start=True, stop=True)
                    ins.then_inc(S["gate_rows"], 1)
                    pe.wait_ge(S["decay_rows"], 1)
                    for j in range(2):
                        ins = pe.matmul(ps[:, 6, HM * j:HM * j + HM], row(5)[:, j * P:j * P + P], ident[0:HM, 0:HM], start=True, stop=True)
                    ins.then_inc(S["gate_cols"], 1)
                    pe.wait_ge(S["v_token_a"], 1)
                    pe.wait_ge(S["v_token_b"], 1)
                elif name == "mlstm":
                    pe.wait_ge(S["chunks_evicted"], (IN0 + 10) * CH + CREDIT)
                    pe.wait_ge(S["gate_cols_read"], 1)

                    def head_row(h):
                        return ident[0:HM, h:h + 1].to_broadcast([HM, P])

                    def scores(h):
                        if h:
                            pe.wait_ge(S["m_scored"], h)
                            pe.wait_ge(S["m_floor"], h)
                        bank = 4 + h % 2
                        pe.matmul(ps[:, bank, 0:T], head_row(h), row(6), start=True, stop=False, skip_group_check=True)
                        pe.matmul(ps[:, bank, 0:P], ident[:, :], shut[:, 0, :], start=False, stop=True, skip_group_check=True)
                        pe.matmul(ps[:, bank, T:T + P], head_row(h), row(6)[:, P:T], start=True, stop=False, skip_group_check=True)
                        pe.matmul(ps[:, bank, T:T + P], ident[:, :], shut[:, 0, :], start=False, stop=True, skip_group_check=True)
                        pe.matmul(ps[:, 3 + 4 * (h // 2), (h % 2) * T:(h % 2) * T + T], head_row(h), row(7), start=True, stop=True)
                        q, k = work[:, h, :], work[:, 4 + h, :]
                        pe.matmul(ps[:, 6, 0:T], k[:, 0:P], q, start=True, stop=True)
                        pe.matmul(ps[:, 6, T:T + P], k[:, P:T], q[:, P:T], start=True, stop=True).then_inc(S["m_scores_raw"], 1)

                    def causal(dst, lhs, score):
                        pe.matmul(dst, lhs[0], score[:, 0:T], start=True, stop=False, skip_group_check=True)
                        return pe.matmul(dst[:, P:T], lhs[1], score[:, T:T + P], start=False, stop=True, skip_group_check=True)

                    def products(h):
                        pe.wait_ge(S["m_scored"], h + 1)
                        if h:
                            pe.wait_ge(S["m_normed"], h)
                        causal(ps[:, 2, (h % 2) * T:(h % 2) * T + T], [ones[:, :]] * 2, m_score(h))
                        for v in range(2):
                            col = h * DV + v * P
                            ins = causal(ps[:, h % 2, v * T:v * T + T], [t[:, col:col + P] for t in vtok], m_score(h))
                        ins.then_inc(S["m_products"], 1)

                    def meansq(h):
                        pe.wait_ge(S["m_squared"], h + 1)
                        pe.wait_ge(S["m_floor"], h // 2 * 2 + 2)
                        dst = ps[:, 3 + 4 * (h // 2), (h % 2) * T:(h % 2) * T + T]
                        sq = m_score(h)
                        pe.matmul(dst, ones[:, :], sq[:, 0:T], start=True, stop=False, skip_group_check=True)
                        pe.matmul(dst, ones[:, :], sq[:, T:2 * T], start=False, stop=True, skip_group_check=True)\
                          .then_inc(S["m_meansq"], 1)

                    scores(0)
                    scores(1)
                    products(0)
                    for h in range(2, HM):
                        scores(h)
                        meansq(h - 2)
                        products(h - 1)
                    meansq(2)
                    products(3)
                    meansq(3)
                    pe.wait_ge(S["m_roots"], 1)
                    pe.wait_ge(S["mixer_low"], 2)
                elif name == "attend":
                    g = c
                    pe.wait_ge(S["chunks_evicted"], (g * 3 + IN1 + 3) * CH + CREDIT)
                    for j in range(2):
                        for h in range(4):
                            ins = pe.transpose(ps[:, j, h * P:h * P + P], work[:, 8 + h, j * P:j * P + P], ident[:, :])
                    ins.then_inc(S["s_v_turned"], 1)
                    pe.wait_ge(S["s_q_scaled"], g + 1)
                    for w in range(2):
                        for h in (2 * w, 2 * w + 1):
                            q, k = work[:, h, :], work[:, 4 + h, :]
                            pe.matmul(ps[:, 4 + h, 0:T], k[:, 0:P], q, start=True, stop=False, skip_group_check=True)
                            ins = pe.matmul(ps[:, 4 + h, T:T + P], k[:, P:T], q[:, P:T], start=False, stop=False,
                                            skip_group_check=True)
                        ins.then_inc(S["s_scores"], 1)
                    for w in range(2):
                        pe.wait_ge(S["s_masked"], (g * 2 + w) * 4 + 4)
                        for h in range(2):
                            z = ps[:, 4 + 2 * w + h, :]
                            soft = s_soft(w)[:, h, :]
                            pe.matmul(z[:, 0:T], tri[:, :], soft[:, 0:T], start=False, stop=False, skip_group_check=True)
                            pe.matmul(z[:, P:T], minus[:, :], soft[:, T:T + P], start=False, stop=False, skip_group_check=True)
                            pe.matmul(z[:, T:T + P], tri[:, :], soft[:, T:T + P], start=False, stop=False, skip_group_check=True)
                            for block in (slice(0, P), slice(T, T + P)):
                                ins = pe.matmul(z[:, block], ident[:, :], shut[:, 1, :], start=False, stop=True, skip_group_check=True)
                        ins.then_inc(S["s_logits"], 1)
                    pe.wait_ge(S["s_v_token"], g + 1)
                    for w in range(2):
                        pe.wait_ge(S["s_probs"], g * 2 + w + 1)
                        for h in range(2):
                            dst = ps[:, 2 + w, h * T:h * T + T]
                            probs = s_tmp(w)[:, h, :]
                            col = (2 * w + h) * P
                            pe.matmul(dst, s_vtok[:, 0, col:col + P], probs[:, 0:T], start=True, stop=False, skip_group_check=True)
                            ins = pe.matmul(dst[:, P:T], s_vtok[:, 1, col:col + P], probs[:, T:T + P], start=False, stop=True,
                                            skip_group_check=True)
                        ins.then_inc(S["s_out"], 1)
                    pe.wait_ge(S["s_low"], g * 2 + 2)

            run_stream(pe, body, between)


def kernel(x, c, ada_w, ada_b, norm_g, final_g, ffn_w1, ffn_w3, ffn_w2, ab_w_in, ab_w_out, lru_conv_w, lru_conv_b,
           lru_gate_w, lru_gate_b, lru_lambda, mlstm_gate_b, mlstm_norm_g, sb_w_qkv, sb_w_out):
    import numpy as np
    import concourse.bacc as bacc
    from concourse.bass_utils import run_bass_kernel_spmd as run

    def chunks(w):
        k, n = w.shape
        return w.reshape(k // P, P, n // P, P).transpose(2, 1, 0, 3).reshape(n // P, P, k)

    x, ada_w, w_in = np.asarray(x), np.asarray(ada_w), np.asarray(ab_w_in)[0]
    w1, w3, w2 = (np.asarray(w) for w in (ffn_w1, ffn_w3, ffn_w2))
    wts = np.zeros((BODIES * CH, P, D), w_in.dtype)
    at = [0]

    def put(c):
        wts[at[0]:at[0] + c.shape[0], :, :c.shape[2]] = c
        at[0] += c.shape[0]

    def put_ffn(layer):
        first = 0
        for n in GROUPS:
            cols = slice(first * P, (first + n) * P)
            put(np.stack([chunks(w1[layer][:, cols]), chunks(w3[layer][:, cols])], axis=1).reshape(2 * n, P, D))
            put(chunks(w2[layer][cols]))
            first += n

    xa, ya, q, k, v, o = np.split(w_in[:, :5120], [1024, 2048, 2560, 3072, 4096], axis=1)
    put(chunks(w_in[:, :5120]))
    put(chunks(np.asarray(ab_w_out)[0]))
    put_ffn(0)
    qkv = np.asarray(sb_w_qkv)[0]
    for g in range(4):
        for j in range(3):
            put(chunks(qkv[:, j * D + g * 512:j * D + g * 512 + 512]))
    put(chunks(np.asarray(sb_w_out)[0]))
    put_ffn(1)

    def cols(a, lead):
        a = np.asarray(a).reshape(lead, -1, P)
        return np.ascontiguousarray(a.transpose(2, 0, 1))

    data = {
        "xT": np.ascontiguousarray(x[0].T.reshape(KT, P, T).transpose(1, 0, 2)),
        "c_row": np.asarray(c).reshape(1, D),
        "wts": wts,
        "ada": np.ascontiguousarray(ada_w.reshape(4, D, 3 * D).transpose(0, 2, 1)).reshape(12 * KT, P, D),
        "ada_b": cols(ada_b, 1)[:, 0, :],
        "norm_g": cols(np.concatenate([np.asarray(norm_g).reshape(4, D), np.asarray(final_g).reshape(1, D)]), 5),
        "wgate": np.ascontiguousarray(w_in[:, 5120:].reshape(KT, P, 8).transpose(1, 0, 2)),
        "conv": np.ascontiguousarray(np.concatenate([np.asarray(lru_conv_w)[0], np.asarray(lru_conv_b)]).reshape(5, LT, P).transpose(2, 1, 0)),
        "lru_w": np.ascontiguousarray(np.asarray(lru_gate_w)[0].transpose(2, 0, 1, 3)).reshape(P, 2 * LT * P),
        "lru_b": cols(np.asarray(lru_gate_b)[0], 2),
        "lam": cols(lru_lambda, 1)[:, 0, :],
        "gate_b": np.ascontiguousarray(np.asarray(mlstm_gate_b)[0].T),
        "mnorm_g": cols(mlstm_norm_g, 1)[:, 0, :],
    }
    data = {name: np.ascontiguousarray(a) for name, a in data.items()}
    nc = bacc.Bacc("TRN2", target_bir_lowering=False, num_devices=1)
    args = {name: nc.dram_tensor(name + "_dram", a.shape, mybir.dt.from_np(a.dtype), kind="ExternalInput").ap()
            for name, a in data.items()}
    out = nc.dram_tensor("out_dram", (P, KT, T), F32, kind="ExternalOutput").ap()
    bass_trunk(nc, out=out, **args)
    r = run(nc, [{name + "_dram": a for name, a in data.items()}], core_ids=[0])
    return r.results[0]["out_dram"].transpose(2, 1, 0).reshape(1, T, D)
```

```python
from contextlib import ExitStack

import concourse.bass as bass
from concourse import mybir

ALU = mybir.AluOpType
ACT = mybir.ActivationFunctionType
AX = mybir.AxisListType
F32 = mybir.dt.float32
F32R = mybir.dt.float32r

P = 128
T = 256
D = 2048
KT = D // P
FFN = 5632
FT = FFN // P
EPS = 1e-6
HM = 4
DK = 128
DV = 256
DH = 128
LT = 8
LRU_C = 8.0
GROUPS = [16, 16, 12]
CH = 4
HALF = D // 2
HK = KT // 2
NEVER = -1e30
CREDIT = 4
EARLY = 2 * KT

UP = [2 * n // CH for n in GROUPS]
DOWN = KT // CH
FFN_BODIES = sum(UP) + DOWN * len(GROUPS)
IN0 = 0
OUT0 = IN0 + 10
FFN0 = OUT0 + DOWN
IN1 = FFN0 + FFN_BODIES
OUT1 = IN1 + 12
FFN1 = OUT1 + DOWN
BODIES = FFN1 + FFN_BODIES
LAST_UPDATE = [None, OUT0, FFN0 + FFN_BODIES - DOWN, OUT1, BODIES - DOWN]
UPDATES = {"out0": 0, "down0": KT, "out1": KT * 4, "down1": KT * 5}


STORED = {"x_branch": (0, 4, 0, 4, 1.0), "y_branch": (8, 4, 8, 4, 1.0), "qk": (0, 4, 16, 4, 1.0),
          "o": (8, 4, 24, 4, 1.0), "q": (0, 0, 32, 8, float(DH) ** -0.5), "k": (4, 0, 36, 8, 1.0)}
TOKENS = ("v", "vs")


def run_stream(eng, body, between):
    def bodies(first, count, kind, pair=0, units=0, q=0, i0=0):
        with eng.Fori(0, count) as i:
            body(i + first, kind, q, i + i0, i * (units // 2) + pair, units)

    def ffn(first, layer):
        up, down = f"up{layer}", f"down{layer}"

        def group(q, pair, units):
            b = q * (UP[0] + DOWN) + first
            peel = 0 if q else 1
            if peel:
                body(b, up, q, 0, pair, units, True)
            with eng.Fori(peel, UP[0]) as i:
                body(b + i, up, q, i, i + pair, units)
            units = 0 if layer else units
            with eng.Fori(0, DOWN) as i:
                body(b + UP[0] + i, down, q, i, i + (pair + UP[0]), units)

        b = first + 2 * (UP[0] + DOWN)
        if layer:
            group(0, 88, 2)
            group(1, 0, 0)
            bodies(b, UP[2], up, q=2)
            bodies(b + UP[2], DOWN - 1, down + "short", q=2)
            body(b + UP[2] + DOWN - 1, down + "short", 2, DOWN - 1, 0, -1)
        else:
            for q in range(2):
                group(q, q * (UP[0] + DOWN) + 40, 2)
            bodies(b, UP[2], up, 64, 2, q=2)
            bodies(b + UP[2], 2, down + "short", 70, 2, q=2)
            bodies(b + UP[2] + 2, DOWN - 2, down + "short", q=2, i0=2)

    between("start", None)
    between("prologue", None)
    between("norm", 0)
    body(IN0, "x_branch", 0, 0, 16, 4, True)
    body(IN0 + 1, "x_branch", 0, 1, 18, 4)
    between("lru", None)
    bodies(IN0 + 2, 2, "y_branch", 20, 4)
    between("gelu", None)
    bodies(IN0 + 4, 2, "qk", 24, 4)
    bodies(IN0 + 6, 2, "v", 28, 4)
    between("gates", None)
    bodies(IN0 + 8, 2, "o", 32, 4)
    between("mlstm", None)
    bodies(OUT0, DOWN, "out0", 36, 2)
    between("norm", 1)
    ffn(FFN0, 0)
    between("norm", 2)
    body(IN1, "q", 0, 0, 72, 2, True)
    with eng.Fori(0, 3) as g:
        b = g * 3 + (IN1 + 1)
        body(b, "k", 0, g, g * 3 + 73, 2)
        between("scores", g)
        body(b + 1, "vs", 0, g, g * 3 + 74, 2)
        between("sums", g)
        body(b + 2, "q", 0, g + 1, g * 3 + 75, 2)
        between("values", g)
    body(IN1 + 10, "k", 0, 3, 82, 2)
    between("scores", 3)
    body(IN1 + 11, "vs", 0, 3, 83, 2)
    between("sums", 3)
    between("values", 3)
    bodies(OUT1, DOWN, "out1", 84, 2)
    between("norm", 3)
    ffn(FFN1, 1)
    between("norm", 4)


def split_lead(n, s):
    return n + (s + 2) // CH, (s + 2) % CH


def bass_trunk(nc, xT, c_row, wts, ada, ada_b, norm_g, wgate, conv, lru_w, lru_b, lam, gate_b, mnorm_g, out):
    with ExitStack() as ctx:
        def sb(name, shape, dt=F32):
            return ctx.enter_context(nc.sbuf_tensor(name, shape, dt))

        def sem(name):
            return ctx.enter_context(nc.semaphore(name))

        ps = ctx.enter_context(nc.psum_tensor("ps", [P, 8, 512], F32))

        x = sb("x", [P, KT, T])
        hn = sb("hn", [P, KT, 2, T], F32R)
        mid = sb("mid", [P, KT, 2, T], F32R)
        raw = sb("raw", [P, CH, D])
        whigh = sb("whigh", [P, 4, HALF], F32R)
        wlow = sb("wlow", [P, 4, HALF], F32R)
        adaw = sb("adaw", [P, 2, D])
        cact = sb("cact", [P, D])
        work = sb("work", [P, 34, T])
        mod = sb("mod", [P, 12 * KT])
        dots = sb("dots", [P, 4])
        gains = sb("gains", [P, 5, KT])
        slope = sb("slope", [P, KT])
        rstd = sb("rstd", [P, T])
        ones = sb("ones", [P, P])
        minus = sb("minus", [P, P])
        ident = sb("ident", [P, P])
        tri = sb("tri", [P, P])
        shut = sb("shut", [P, 2, P])
        epsb = sb("epsb", [P, 1])
        convw = sb("convw", [P, LT, 5])
        lrub = sb("lrub", [P, 2, LT])
        lamb = sb("lamb", [P, LT])
        lamt = sb("lamt", [P, 4, LT])
        lruc = sb("lruc", [P, 2, LT])
        mng = sb("mng", [P, 8])
        gb = sb("gb", [HM, 2])
        gtok = sb("gtok", [P, 2, 8])
        gcol = sb("gcol", [P, 2, HM])

        weight_loaded = [sem(f"weight_loaded{s}") for s in range(CH)]
        ada_loaded = [sem(f"ada_loaded{s}") for s in range(2)]
        names = """c_loaded norm_consts_loaded x_loaded small_loaded lru_w_loaded stored
            high_ready low_ready halves_multiplied chunks_evicted half_added half_stored
            unit_done mod_added c_ready consts_ready
            square_step variance_ready std_ready rstd_ready slope_ready scaled_ready
            hn_high_ready hn_ready final_ready
            silu_ready hidden_product hidden_high hidden_ready
            gate_w_high gate_w_ready lam_abs lam_exp lam_ready
            conv_ready lru_gates_ready lru_a_ready lru_in_gated lru_root_in lru_roots lru_state gelu_ready
            mixer_low
            gates_summed gate_tokens gate_rows forget_abs forget_exp forget_log
            decay_rows gate_cols gate_cols_read m_scores_raw m_weights m_floor m_scored m_products m_den_abs m_normed
            m_squared m_meansq m_roots m_rstd o_ready m_out m_high
            s_scores s_abs s_exp1 s_log s_softplus s_masked s_logits s_probs
            s_out s_high s_low dve_chain act_chain pool_chain""".split()
        S = {n: sem(n) for n in names}

        XA, XC, GW, W8 = (work[:, i:i + 8, :] for i in (0, 8, 16, 24))

        def flat(ap):
            return ap.rearrange("p a t -> p (a t)")

        def work_tile(i):
            return flat(work[:, bass.ds(i, 1), :])

        vtok = [flat(work[:, 16 + 4 * j:20 + 4 * j, :]) for j in range(2)]

        def m_weight(h):
            return flat(work[:, 24:27, :])[:, (h % 2) * (T + P):(h % 2 + 1) * (T + P)]

        def m_score(h):
            return flat(work[:, 27 + 2 * (h % 2):29 + 2 * (h % 2), :])

        def m_floor_row(h):
            return rstd[:, :] if h % 2 else work[:, 31, :]

        s_vtok = flat(work[:, 12:16, :]).rearrange("p (j n) -> p j n", j=2)

        def s_soft(w):
            return flat(work[:, 16 + 3 * w:19 + 3 * w, :]).rearrange("p (h n) -> p h n", h=2)

        def s_tmp(w):
            return flat(work[:, 22 + 3 * w:25 + 3 * w, :]).rearrange("p (h n) -> p h n", h=2)

        def row(i):
            return work[0:HM, 26 + i, :]

        squares_sum = work[:, 31, :]
        square = work[:, 32, :]
        wg = mid[:, KT - 1, 0, :].rearrange("p (k h g) -> p k h g", k=KT, h=2)
        wg_raw = work[:, 30, 0:8 * KT].rearrange("p (k g) -> p k g", g=8)

        def mod_vec(i, m=slice(0, KT)):
            return mod[:, i * KT:i * KT + KT][:, m]

        def units_count(v):
            return (v + 1) * KT

        def unit_place(u):
            slot = u % 4
            if slot < 2:
                return adaw[:, slot, :], ada_loaded[slot], u // 4
            return raw[:, slot, :], weight_loaded[slot], u // 4

        EARLY_LOADS = EARLY // 4

        def weight_count(n, s):
            return (n + (EARLY_LOADS if s >= 2 else 0)) * 16 + 16

        block = ctx.enter_context(nc.Block())

        @block.sync
        def _(sp):
            sp.dma_start(cact[:, :], c_row.to_broadcast([P, D])).then_inc(S["c_loaded"], 16)
            sp.dma_start(mod[:, :], ada_b).then_inc(S["norm_consts_loaded"], 16)
            sp.dma_start(gains[:, :, :], norm_g).then_inc(S["norm_consts_loaded"], 16)

            def body(n, kind, q, i, pair, units, fresh=False):
                for s in range(CH):
                    if units >= 0:
                        sp.wait_ge(S["low_ready"], n * 8 + 2 * s + 2)
                        sp.dma_start(raw[:, s, :], wts[bass.ds(n * CH + s + CH, 1), :, :].rearrange("a p n -> p (a n)"))\
                          .then_inc(weight_loaded[s], 16)
                    for u in range(s * units // CH, (s + 1) * units // CH):
                        sp.wait_ge(S["unit_done"], pair * 2 + u + 1)
                        sp.dma_start(adaw[:, u % 2, :], ada[bass.ds(pair * 2 + u, 1), :, :].rearrange("a p n -> p (a n)"))\
                          .then_inc(ada_loaded[u % 2], 16)

            def between(name, c):
                if name == "prologue":
                    for u in range(EARLY):
                        place, loaded, before = unit_place(u)
                        if before:
                            sp.wait_ge(S["unit_done"], u - 4 + 3)
                        sp.dma_start(place, ada[u, :, :]).then_inc(loaded, 16)
                        if u == 1:
                            sp.dma_start(x[:, :, :], xT).then_inc(S["x_loaded"], 16)
                        if u == 3:
                            for s in range(2):
                                sp.dma_start(raw[:, s, :], wts[s, :, :]).then_inc(weight_loaded[s], 16)
                    for s in range(2, CH):
                        sp.wait_ge(S["unit_done"], EARLY - CH + s + 3)
                        sp.dma_start(raw[:, s, :], wts[s, :, :]).then_inc(weight_loaded[s], 16)
                if name == "norm" and c == 4:
                    for j in range(4):
                        sp.wait_ge(S["final_ready"], 4 * j + 4)
                        sp.dma_start(out[:, 4 * j:4 * j + 4, :], x[:, 4 * j:4 * j + 4, :]).then_inc(S["stored"], 16)
                    sp.wait_ge(S["stored"], 64)

            run_stream(sp, body, between)

        @block.gpsimd
        def _(pool):
            pool.memset(ones[:, :], 1.0).then_inc(S["pool_chain"], 1)
            pool.memset(minus[:, :], -1.0).then_inc(S["pool_chain"], 1)
            pool.memset(epsb[:, :], EPS).then_inc(S["consts_ready"], 1)
            pool.memset(shut[:, :, :], NEVER).then_inc(S["pool_chain"], 1)
            pool.wait_ge(S["pool_chain"], 3)
            pool.affine_select(out=ident[:, :], in_=ones[:, :], compare_op=ALU.is_equal, fill=0.0, base=0,
                               pattern=[[-1, P]], channel_multiplier=1).then_inc(S["consts_ready"], 1)
            pool.affine_select(out=tri[:, :], in_=minus[:, :], compare_op=ALU.is_ge, fill=0.0, base=0,
                               pattern=[[-1, P]], channel_multiplier=1).then_inc(S["consts_ready"], 1)
            for j, compare in enumerate((ALU.is_gt, ALU.is_ge)):
                pool.affine_select(out=shut[:, j, :], in_=shut[:, j, :], compare_op=compare, fill=0.0, base=0,
                                   pattern=[[-1, P]], channel_multiplier=1).then_inc(S["consts_ready"], 1)

            def squares(norm):
                if norm:
                    pool.wait_ge(S["variance_ready"], norm)
                    pool.wait_ge(S["chunks_evicted"], LAST_UPDATE[norm] * CH + 1 + CREDIT)
                else:
                    pool.wait_ge(S["x_loaded"], 16)
                pool.memset(squares_sum, 0.0).then_inc(S["square_step"], 1)
                with pool.Fori(0, KT) as m:
                    xm = x[:, bass.ds(m, 1), :].rearrange("p a t -> p (a t)")
                    if norm:
                        pool.wait_ge(S["chunks_evicted"], m + LAST_UPDATE[norm] * CH + 1 + CREDIT)
                    pool.wait_ge(S["square_step"], m * 2 + 33 * norm + 1)
                    pool.tensor_tensor(square, xm, xm, ALU.mult).then_inc(S["square_step"], 1)
                    pool.wait_ge(S["square_step"], m * 2 + 33 * norm + 2)
                    pool.tensor_tensor(squares_sum, squares_sum, square, ALU.add).then_inc(S["square_step"], 1)

            def between(name, c):
                if name == "norm":
                    squares(c)
                elif name == "scores":
                    for w in range(2):
                        pool.wait_ge(S["s_softplus"], c * 2 + w + 1)
                        for h in range(2):
                            for block in (slice(0, P), slice(T, T + P)):
                                m = s_soft(w)[:, h, block]
                                pool.affine_select(out=m, in_=m, compare_op=ALU.is_gt, fill=0.0, base=0,
                                                   pattern=[[1, P]], channel_multiplier=-1).then_inc(S["s_masked"], 1)

            between("norm", 0)
            between("norm", 1)
            between("norm", 2)
            for g in range(4):
                between("scores", g)
            between("norm", 3)
            between("norm", 4)

        @block.scalar
        def _(act):
            def split(n, s):
                act.wait_ge(weight_loaded[s], weight_count(n, s))
                for h in range(2):
                    act.wait_ge(S["halves_multiplied"], n * 8 + 2 * s + h + 1)
                    act.activation(whigh[:, (2 * s + h) % 4, :], raw[:, s, h * HALF:(h + 1) * HALF], ACT.Copy)\
                       .then_inc(S["high_ready"], 1)

            def body(n, kind, q, i, pair, units, fresh=False):
                for s in range(CH):
                    if units >= 0 or s < 2:
                        split(*split_lead(n, s))
                    if kind in STORED:
                        first, tiles, number, numbers, factor = STORED[kind]
                        act.wait_ge(S["halves_multiplied"], n * 8 + 2 * s + 2 + CREDIT)
                        act.activation(work_tile(i * tiles + (first + s)), ps[:, s, T:2 * T], ACT.Copy, scale=factor)\
                           .then_inc(S["half_stored"], 1)
                    if kind[:2] == "up" and s % 2:
                        act.wait_ge(S["chunks_evicted"], n * CH + s + CREDIT)
                        act.activation(work[:, 2 + s // 2, :], work[:, s // 2, :], ACT.Silu).then_inc(S["silu_ready"], 1)

            def norm(i):
                act.wait_ge(S["variance_ready"], i + 1)
                act.wait_ge(S["consts_ready"], 5)
                if i:
                    act.wait_ge(S["hn_ready"], KT * i)
                act.activation(rstd[:, :], ps[:, 7, 0:T], ACT.Sqrt, scale=1.0 / D, bias=epsb[:, 0:1]).then_inc(S["std_ready"], 1)
                if i < 4:
                    for k in range(KT):
                        act.wait_ge(S["scaled_ready"], KT * i + k + 1)
                        act.activation(hn[:, k, 0, :], work[:, k, :], ACT.Identity, bias=mod_vec(3 * i)[:, k:k + 1])\
                           .then_inc(S["hn_high_ready"], 1)

            def between(name, c):
                if name == "start":
                    act.wait_ge(S["c_loaded"], 16)
                    act.activation(cact[:, :], cact[:, :], ACT.Silu).then_inc(S["c_ready"], 1)
                    for dst, src in ((wg_raw[:, :, :], wgate), (convw[:, :, :], conv), (lrub[:, :, :], lru_b), (lamb[:, :], lam),
                                     (gb[:, :], gate_b), (mng[:, :], mnorm_g)):
                        act.dma_start(dst, src).then_inc(S["small_loaded"], 16)
                    act.dma_start(flat(GW), lru_w).then_inc(S["lru_w_loaded"], 16)
                    act.wait_ge(S["small_loaded"], 16 * 6)
                    act.activation(wg[:, :, 0, :], wg_raw[:, :, :], ACT.Copy).then_inc(S["gate_w_high"], 1)
                    act.wait_ge(S["lam_abs"], 1)
                    act.activation(lamt[:, 1, :], lamt[:, 0, :], ACT.Exp, scale=-1.0).then_inc(S["lam_exp"], 1)
                elif name == "norm" and c:
                    norm(c)
                elif name == "prologue":
                    split(0, 0)
                    split(0, 1)
                    norm(0)
                elif name == "lru":
                    act.wait_ge(S["lam_ready"], 1)
                    for n in range(LT):
                        bank = ps[:, 4 + n % 2, :]
                        act.wait_ge(S["lru_gates_ready"], n + 1)
                        act.activation(W8[:, n, :], bank[:, 0:T], ACT.Tanh, scale=0.5,
                                       bias=lrub[:, 0, n:n + 1]).then_inc(S["act_chain"], 1)
                        act.activation(bank[:, T:2 * T], bank[:, T:2 * T], ACT.Tanh, scale=0.5,
                                       bias=lrub[:, 1, n:n + 1])
                        act.wait_ge(S["act_chain"], 2 * n + 1)
                        act.activation(XA[:, n, :], W8[:, n, :], ACT.Exp, scale=lruc[:, 0, n:n + 1],
                                       bias=lruc[:, 0, n:n + 1]).then_inc(S["act_chain"], 1)
                        act.wait_ge(S["act_chain"], 2 * n + 2)
                        act.activation(W8[:, n, :], W8[:, n, :], ACT.Tanh, scale=lruc[:, 1, n:n + 1],
                                       bias=lruc[:, 1, n:n + 1]).then_inc(S["lru_a_ready"], 1)
                    act.wait_ge(S["lru_root_in"], LT)
                    act.activation(flat(W8), flat(W8), ACT.Sqrt).then_inc(S["lru_roots"], 1)
                    act.wait_ge(S["lru_state"], LT)
                elif name == "gelu":
                    act.wait_ge(S["chunks_evicted"], (IN0 + 4) * CH + CREDIT)
                    act.activation(flat(XC), flat(XC), ACT.Gelu_apprx_tanh).then_inc(S["gelu_ready"], 1)
                elif name == "gates":
                    act.wait_ge(S["forget_abs"], 1)
                    act.activation(row(2), row(1), ACT.Exp, scale=-1.0).then_inc(S["forget_exp"], 1)
                    act.wait_ge(S["forget_exp"], 1)
                    act.activation(row(2), row(2), ACT.Ln, bias=ones[0:HM, 0:1]).then_inc(S["forget_log"], 1)
                elif name == "mlstm":
                    def squared(h):
                        den = ps[:, 2, (h % 2) * T:(h % 2) * T + T]
                        act.wait_ge(S["m_products"], h + 1)
                        act.activation(den, den, ACT.Abs).then_inc(S["m_den_abs"], 1)
                        act.wait_ge(S["m_normed"], h + 1)
                        act.activation(m_score(h), work[:, h:h + 5:4, :], ACT.Square).then_inc(S["m_squared"], 1)

                    for h in range(HM):
                        bank = ps[:, 4 + h % 2, :]
                        act.wait_ge(S["m_scores_raw"], h + 1)
                        act.wait_ge(S["gate_cols_read"], 1)
                        if h >= 2:
                            act.wait_ge(S["m_scored"], h - 1)
                            act.wait_ge(S["m_normed"], h - 1)
                        act.activation(m_weight(h)[:, 0:T], bank[:, 0:T], ACT.Exp, bias=gcol[:, 0, h:h + 1])
                        act.activation(m_weight(h)[:, T:T + P], bank[:, T:T + P], ACT.Exp, bias=gcol[:, 1, h:h + 1])\
                           .then_inc(S["m_weights"], 1)
                        act.activation(m_floor_row(h), ps[:, 3 + 4 * (h // 2), (h % 2) * T:(h % 2) * T + T], ACT.Exp).then_inc(S["m_floor"], 1)
                        if h:
                            squared(h - 1)
                    squared(HM - 1)
                    act.activation(flat(XC), flat(XC), ACT.Tanh, scale=0.5).then_inc(S["o_ready"], 1)
                    act.wait_ge(S["m_meansq"], HM)
                    act.activation(work[:, 24:28, :], ps[:, 3:8:4, :], ACT.Sqrt, scale=1.0 / DV, bias=epsb[:, 0:1])\
                       .then_inc(S["m_roots"], 1)
                    act.wait_ge(S["m_out"], 8)
                    act.activation(mid[:, 8:16, 0, :], XC[:, :, :], ACT.Copy).then_inc(S["m_high"], 1)
                elif name == "scores":
                    for w in range(2):
                        act.wait_ge(S["s_scores"], c * 2 + w + 1)
                        act.activation(s_tmp(w), ps[:, 4 + 2 * w:6 + 2 * w, 0:T + P], ACT.Abs).then_inc(S["s_abs"], 1)
                        act.wait_ge(S["s_abs"], c * 2 + w + 1)
                        act.activation(s_tmp(w), s_tmp(w), ACT.Exp, scale=-1.0).then_inc(S["s_exp1"], 1)
                        act.wait_ge(S["s_exp1"], c * 2 + w + 1)
                        act.activation(s_tmp(w), s_tmp(w), ACT.Ln, bias=ones[:, 0:1]).then_inc(S["s_log"], 1)
                elif name == "sums":
                    for w in range(2):
                        act.wait_ge(S["s_logits"], c * 2 + w + 1)
                        act.activation(s_tmp(w), ps[:, 4 + 2 * w:6 + 2 * w, 0:T + P], ACT.Exp).then_inc(S["s_probs"], 1)
                elif name == "values":
                    for w in range(2):
                        act.wait_ge(S["s_out"], c * 2 + w + 1)
                        act.activation(mid[:, bass.ds(c * 4 + 2 * w, 2), 0, :],
                                       ps[:, 4 + 2 * w, :].rearrange("p (h t) -> p h t", h=2), ACT.Copy).then_inc(S["s_high"], 1)

            run_stream(act, body, between)

        @block.vector
        def _(dve):
            links = [0]

            def link(ins):
                links[0] += 1
                ins.then_inc(S["dve_chain"], 1)
                dve.wait_ge(S["dve_chain"], links[0])

            def split(n, s):
                for h in range(2):
                    dve.wait_ge(S["high_ready"], n * 8 + 2 * s + h + 1)
                    half = (2 * s + h) % 4
                    dve.tensor_tensor(wlow[:, half, :], raw[:, s, h * HALF:(h + 1) * HALF], whigh[:, half, :].bitcast(F32),
                                      ALU.subtract).then_inc(S["low_ready"], 1)

            def add_unit(place, u, first):
                if u == 0 and first is not None:
                    dve.wait_ge(S["mod_added"], first)
                dve.tensor_tensor_reduce(out=place, in0=place, in1=cact[:, :], scale=1.0, scalar=0.0, op0=ALU.mult,
                                         op1=ALU.add, accum_out=dots[:, u:u + 1]).then_inc(S["unit_done"], 1)

            def add_to_mod(first, units):
                dve.wait_ge(S["unit_done"], first + units + 2)
                columns = mod[:, bass.ds(first, units)]
                dve.tensor_tensor(columns, columns, dots[:, 0:units], ALU.add).then_inc(S["mod_added"], units)

            def units_of(pair, units, s):
                for u in range(s * units // CH, (s + 1) * units // CH):
                    dve.wait_ge(ada_loaded[u % 2], (pair + (u // 2 - EARLY // 2 + EARLY_LOADS)) * 16 + 16)
                    add_unit(adaw[:, u % 2, :], u, pair * 2)

            def halves_sum(s):
                return ps[:, s, :].rearrange("p (h t) -> p t h", h=2)

            def sum_halves(dst, s):
                dve.tensor_reduce(dst, halves_sum(s), AX.X, ALU.add).then_inc(S["chunks_evicted"], 1)

            def update_x(n, s, kind, q, i):
                norm = {"out0": 0, "down0": 1, "out1": 2, "down1": 3}[kind]
                count = q * KT + i * CH + UPDATES[kind] + s
                m = bass.ds(i * CH + s, 1)
                gate = mod[:, bass.ds(i * CH + (s + (3 * norm + 2) * KT), 1)]
                dve.wait_ge(S["mod_added"], units_count(3 * norm + 2))
                tmp = work[:, 8 + s, :]
                xm = x[:, m, :].rearrange("p a t -> p (a t)")
                dve.scalar_tensor_tensor(tmp, ps[:, s, 0:T], gate, xm, ALU.mult, ALU.add).then_inc(S["half_added"], 1)
                dve.wait_ge(S["half_added"], count + 1)
                dve.scalar_tensor_tensor(xm, ps[:, s, T:2 * T], gate, tmp, ALU.mult, ALU.add).then_inc(S["chunks_evicted"], 1)

            def body(n, kind, q, i, pair, units, fresh=False):
                for s in range(CH):
                    if units >= 0 or s < 2:
                        split(*split_lead(n, s))
                    dve.wait_ge(S["halves_multiplied"], n * 8 + 2 * s + 2 + CREDIT)
                    if kind in STORED:
                        first, tiles, number, numbers, factor = STORED[kind]
                        dst = work_tile(i * tiles + (first + s))
                        dve.wait_ge(S["half_stored"], i * numbers + (number + s + 1))
                        dve.scalar_tensor_tensor(dst, ps[:, s, 0:T], factor, dst, ALU.mult, ALU.add).then_inc(S["chunks_evicted"], 1)
                    elif kind in TOKENS:
                        if s < 2:
                            dve.wait_ge(S["chunks_evicted"], n * CH + s + CREDIT)
                            dve.sem_inc(S["chunks_evicted"], 1)
                        elif s == 3:
                            for j in range(2):
                                dst = s_vtok[:, j, :] if kind == "vs" else vtok[j][:, bass.ds(i * 512, 512)]
                                dve.tensor_copy(dst, ps[:, 2 + j, :]).then_inc(S["chunks_evicted"], 1)
                    elif kind[:2] == "up":
                        j = s // 2
                        if s % 2 == 0:
                            sum_halves(work[:, j, :], s)
                            units_of(pair, units, s)
                        else:
                            layer = int(kind[2])
                            tile = i * 2 + j
                            count = q * GROUPS[0] + i * 2 + (layer * FT + j)
                            sum_halves(work[:, 4 + j, :], s)
                            units_of(pair, units, s)
                            dve.wait_ge(S["silu_ready"], count + 1)
                            dve.wait_ge(S["chunks_evicted"], n * CH + s + 1 + CREDIT)
                            dve.tensor_tensor(work[:, 6 + j, :], work[:, 2 + j, :], work[:, 4 + j, :], ALU.mult)\
                               .then_inc(S["hidden_product"], 1)
                            dve.wait_ge(S["hidden_product"], count + 1)
                            high = mid[:, bass.ds(tile, 1), 0, :].rearrange("p a t -> p (a t)")
                            low = mid[:, bass.ds(tile, 1), 1, :].rearrange("p a t -> p (a t)")
                            dve.tensor_copy(high, work[:, 6 + j, :]).then_inc(S["hidden_high"], 1)
                            dve.wait_ge(S["hidden_high"], count + 1)
                            dve.tensor_tensor(low, work[:, 6 + j, :], high.bitcast(F32), ALU.subtract).then_inc(S["hidden_ready"], 1)
                    else:
                        update_x(n, s, kind.replace("short", ""), q, i)
                    if kind[:2] != "up":
                        units_of(pair, units, s)
                if units > 0:
                    add_to_mod(pair * 2, units)

            def mixer_constants():
                dve.wait_ge(S["small_loaded"], 16 * 6)
                dve.scalar_tensor_tensor(lamt[:, 0, :], lamb[:, :], -1.0, lamb[:, :], ALU.mult, ALU.max).then_inc(S["lam_abs"], 1)
                dve.wait_ge(S["gate_w_high"], 1)
                dve.tensor_tensor(wg[:, :, 1, :], wg_raw[:, :, :], wg[:, :, 0, :].bitcast(F32), ALU.subtract)\
                   .then_inc(S["gate_w_ready"], 1)
                dve.tensor_scalar(lrub[:, :, :], lrub[:, :, :], 0.5, None, ALU.mult)
                dve.tensor_scalar(mng[:, :], mng[:, :], 0.5, None, ALU.mult)
                dve.wait_ge(S["lam_exp"], 1)
                e, t, s, s2 = lamt[:, 1, :], lamt[:, 2, :], lamt[:, 0, :], lamt[:, 3, :]
                link(dve.tensor_scalar(t, e, 2.0, None, ALU.add))
                link(dve.reciprocal(t, t))
                link(dve.tensor_tensor(s, e, t, ALU.mult))
                link(dve.tensor_tensor(s2, s, s, ALU.mult))
                link(dve.tensor_scalar(t, s2, 1.0 / 15, None, ALU.mult))
                for k in (13, 11, 9, 7, 5, 3):
                    link(dve.scalar_tensor_tensor(t, t, 1.0 / k, s2, ALU.add, ALU.mult))
                link(dve.scalar_tensor_tensor(t, t, 1.0, s, ALU.add, ALU.mult))
                link(dve.tensor_scalar(s2, lamb[:, :], 0.0, None, ALU.min))
                link(dve.scalar_tensor_tensor(t, t, -2.0, s2, ALU.mult, ALU.add))
                dve.tensor_scalar(lruc[:, 0, :], t, LRU_C / 2, None, ALU.mult)
                dve.tensor_scalar(lruc[:, 1, :], t, -LRU_C / 2, None, ALU.mult).then_inc(S["lam_ready"], 1)

            def rstd_of(i):
                dve.wait_ge(S["std_ready"], i + 1)
                dve.reciprocal(rstd[:, :], rstd[:, :]).then_inc(S["rstd_ready"], 1)
                dve.wait_ge(S["rstd_ready"], i + 1)

            def scaled(i, k):
                dve.scalar_tensor_tensor(work[:, k, :], x[:, k, :], slope[:, k:k + 1], rstd[:, :], ALU.mult, ALU.mult)\
                   .then_inc(S["scaled_ready"], 1)

            def low(i, k):
                dve.wait_ge(S["hn_high_ready"], KT * i + k + 1)
                dve.scalar_tensor_tensor(hn[:, k, 1, :], work[:, k, :], mod_vec(3 * i)[:, k:k + 1],
                                         hn[:, k, 0, :].bitcast(F32), ALU.add, ALU.subtract).then_inc(S["hn_ready"], 1)

            def norm(i):
                if i < 4:
                    dve.wait_ge(S["mod_added"], units_count(3 * i + 1))
                    dve.scalar_tensor_tensor(slope[:, :], mod_vec(3 * i + 1), 1.0, gains[:, i, :], ALU.add, ALU.mult)\
                       .then_inc(S["slope_ready"], 1)
                rstd_of(i)
                if i == 4:
                    for k in range(KT):
                        dve.scalar_tensor_tensor(x[:, k, :], x[:, k, :], gains[:, 4, k:k + 1], rstd[:, :],
                                                 ALU.mult, ALU.mult).then_inc(S["final_ready"], 1)
                    return
                dve.wait_ge(S["slope_ready"], i + KT)
                for k in range(KT):
                    scaled(i, k)
                    if k:
                        low(i, k - 1)
                low(i, KT - 1)

            def between(name, c):
                if name == "start":
                    dve.sem_inc(S["unit_done"], 2)
                    dve.sem_inc(S["chunks_evicted"], CREDIT)
                    dve.sem_inc(S["s_low"], 2)
                    dve.wait_ge(S["norm_consts_loaded"], 32)
                    dve.wait_ge(S["c_ready"], 1)
                elif name == "prologue":
                    normed = 0
                    for k in range(KT):
                        if k == 3:
                            mixer_constants()
                            split(0, 0)
                            split(0, 1)
                        for u in (2 * k, 2 * k + 1):
                            place, loaded, before = unit_place(u)
                            dve.wait_ge(loaded, before * 16 + 16)
                            add_unit(place, u % 4, u or None)
                        columns = mod[:, k:k + KT + 1:KT]
                        dve.wait_ge(S["unit_done"], 2 * k + 2 + 2)
                        dve.tensor_tensor(columns, columns, dots[:, u % 4 - 1:u % 4 + 1], ALU.add).then_inc(S["mod_added"], 2)
                        dve.wait_ge(S["mod_added"], 2 * k + 2)
                        dve.scalar_tensor_tensor(slope[:, k:k + 1], mod_vec(1)[:, k:k + 1], 1.0, gains[:, 0, k:k + 1],
                                                 ALU.add, ALU.mult).then_inc(S["slope_ready"], 1)
                        if k == 7:
                            rstd_of(0)
                        for _ in range(2 if k >= 7 else 0):
                            if normed <= k:
                                dve.wait_ge(S["slope_ready"], normed + 1)
                                scaled(0, normed)
                                if normed:
                                    low(0, normed - 1)
                                normed += 1
                    low(0, KT - 1)
                elif name == "norm" and c:
                    norm(c)
                elif name == "lru":
                    dve.wait_ge(S["chunks_evicted"], (IN0 + 2) * CH + CREDIT)
                    for n in range(LT):
                        link(dve.tensor_scalar(XC[:, n, :], XA[:, n, :], convw[:, n, 3:4], convw[:, n, 4:5], ALU.mult, ALU.add))
                        for back in (1, 2, 3):
                            ins = dve.scalar_tensor_tensor(XC[:, n, back:T], XA[:, n, 0:T - back], convw[:, n, 3 - back:4 - back],
                                                           XC[:, n, back:T], ALU.mult, ALU.add)
                            if back < 3:
                                link(ins)
                        ins.then_inc(S["conv_ready"], 1)
                    for n in range(LT):
                        bank = ps[:, 4 + n % 2, :]
                        dve.wait_ge(S["lru_a_ready"], n + 1)
                        dve.wait_ge(S["conv_ready"], LT)
                        dve.scalar_tensor_tensor(XC[:, n, :], bank[:, T:2 * T], 1.0, XC[:, n, :], ALU.add, ALU.mult)\
                           .then_inc(S["lru_in_gated"], 1)
                        link(dve.tensor_tensor(bank[:, 0:T], XA[:, n, :], XA[:, n, :], ALU.mult))
                        dve.scalar_tensor_tensor(W8[:, n, :], bank[:, 0:T], 1.0, W8[:, n, :], ALU.add, ALU.mult)\
                           .then_inc(S["lru_root_in"], 1)
                    dve.wait_ge(S["lru_roots"], 1)
                    dve.wait_ge(S["lru_in_gated"], LT)
                    link(dve.scalar_tensor_tensor(flat(XC), flat(W8), 0.5, flat(XC), ALU.mult, ALU.mult))
                    for n in range(LT):
                        dve.tensor_tensor_scan(W8[:, n, :], XA[:, n, :], XC[:, n, :], 0.0, ALU.mult, ALU.add)\
                           .then_inc(S["lru_state"], 1)
                    dve.wait_ge(S["lru_state"], LT)
                elif name == "gelu":
                    dve.wait_ge(S["gelu_ready"], 1)
                    link(dve.tensor_tensor(flat(W8), flat(W8), flat(XC), ALU.mult))
                    link(dve.tensor_copy(mid[:, 0:8, 0, :], W8[:, :, :]))
                    dve.tensor_tensor(mid[:, 0:8, 1, :], W8[:, :, :], mid[:, 0:8, 0, :].bitcast(F32), ALU.subtract)\
                       .then_inc(S["mixer_low"], 1)
                    dve.wait_ge(S["mixer_low"], 1)
                elif name == "gates":
                    dve.wait_ge(S["gates_summed"], 1)
                    for j in range(2):
                        ins = dve.tensor_reduce(gtok[:, j, :], ps[:, 5, 16 * j:16 * j + 16].rearrange("p (h t) -> p t h", h=2),
                                                AX.X, ALU.add)
                    ins.then_inc(S["gate_tokens"], 1)
                    dve.wait_ge(S["gate_rows"], 1)
                    dve.tensor_scalar(row(3), ps[0:HM, 4, 0:T], gb[:, 0:1], None, ALU.add)
                    dve.memset(row(4), 0.0)
                    link(dve.tensor_scalar(row(0), ps[0:HM, 4, T:2 * T], gb[:, 1:2], None, ALU.add))
                    dve.scalar_tensor_tensor(row(1), row(0), -1.0, row(0), ALU.mult, ALU.max).then_inc(S["forget_abs"], 1)
                    link(dve.tensor_scalar(row(0), row(0), 0.0, None, ALU.min))
                    dve.wait_ge(S["forget_log"], 1)
                    link(dve.tensor_tensor(row(0), row(0), row(2), ALU.subtract))
                    dve.wait_ge(S["consts_ready"], 5)
                    link(dve.tensor_tensor_scan(row(2), row(0), row(4), 0.0, ALU.add, ALU.add))
                    link(dve.tensor_tensor(row(5), row(3), row(2), ALU.subtract))
                    link(dve.tensor_tensor_scan(row(1), row(5), row(5), 0.0, ALU.max, ALU.max))
                    dve.tensor_scalar(row(6), row(1), -1.0, None, ALU.mult)
                    dve.scalar_tensor_tensor(row(7), row(2), -1.0, row(1), ALU.mult, ALU.subtract)\
                       .then_inc(S["decay_rows"], 1)
                    dve.wait_ge(S["gate_cols"], 1)
                    dve.tensor_copy(gcol[:, :, :], ps[:, 6, 0:2 * HM].rearrange("p (a h) -> p a h", a=2)).then_inc(S["gate_cols_read"], 1)
                elif name == "mlstm":
                    def scored(h):
                        dve.wait_ge(S["m_weights"], h + 1)
                        if h >= 2:
                            dve.wait_ge(S["m_meansq"], h - 1)
                        dve.scalar_tensor_tensor(m_score(h)[:, 0:T + P], ps[:, 6, 0:T + P], float(DK) ** -0.5,
                                                 m_weight(h)[:, 0:T + P], ALU.mult, ALU.mult).then_inc(S["m_scored"], 1)

                    def normed(h):
                        f = m_floor_row(h)
                        dve.wait_ge(S["m_den_abs"], h + 1)
                        link(dve.tensor_tensor(f, ps[:, 2, (h % 2) * T:(h % 2) * T + T], f, ALU.max))
                        link(dve.reciprocal(f, f))
                        dve.tensor_tensor(work[:, h:h + 5:4, :], ps[:, h % 2, :].rearrange("p (a t) -> p a t", a=2),
                                          f.rearrange("p (a t) -> p a t", a=1).to_broadcast([P, 2, T]), ALU.mult)\
                           .then_inc(S["m_normed"], 1)

                    scored(0)
                    for h in range(1, HM):
                        scored(h) if h == 1 else None
                        normed(h - 1)
                        if h + 1 < HM:
                            scored(h + 1)
                    normed(HM - 1)
                    dve.wait_ge(S["o_ready"], 1)
                    dve.wait_ge(S["m_normed"], HM)
                    for v in range(2):
                        o = XC[:, v:8:2, :]
                        ins = dve.scalar_tensor_tensor(o, o, 1.0, work[:, 4 * v:4 * v + 4, :], ALU.add, ALU.mult)
                    link(ins)
                    dve.wait_ge(S["m_roots"], 1)
                    link(dve.reciprocal(flat(work[:, 24:28, :]), flat(work[:, 24:28, :])))
                    for j in range(8):
                        dve.scalar_tensor_tensor(XC[:, j, :], XC[:, j, :], mng[:, j:j + 1], work[:, 24 + j // 2, :],
                                                 ALU.mult, ALU.mult).then_inc(S["m_out"], 1)
                    dve.wait_ge(S["m_high"], 1)
                    dve.tensor_tensor(mid[:, 8:16, 1, :], XC[:, :, :], mid[:, 8:16, 0, :].bitcast(F32), ALU.subtract)\
                       .then_inc(S["mixer_low"], 1)
                elif name == "scores":
                    for w in range(2):
                        z = ps[:, 4 + 2 * w:6 + 2 * w, 0:T + P]
                        dve.wait_ge(S["s_log"], c * 2 + w + 1)
                        dve.scalar_tensor_tensor(s_soft(w), z, 0.0, s_tmp(w), ALU.max, ALU.add).then_inc(S["s_softplus"], 1)
                elif name == "values":
                    for w in range(2):
                        dve.wait_ge(S["s_high"], c * 2 + w + 1)
                        m = mid[:, bass.ds(c * 4 + 2 * w, 2), :, :]
                        dve.tensor_tensor(m[:, :, 1, :], ps[:, 4 + 2 * w, :].rearrange("p (h t) -> p h t", h=2),
                                          m[:, :, 0, :].bitcast(F32), ALU.subtract).then_inc(S["s_low"], 1)

            run_stream(dve, body, between)

        @block.tensor
        def _(pe):
            def fresh_half(n, kind):
                norm = {"x_branch": 0, "up0": 1, "q": 2, "up1": 3}[kind]
                pe.wait_ge(S["chunks_evicted"], n * CH + 2)
                pe.wait_ge(S["low_ready"], n * 8 + 4)
                for kk in range(KT):
                    pe.wait_ge(S["hn_ready"], KT * norm + kk + 1)
                    w = slice(kk % HK * P, kk % HK * P + P)
                    for s in range(2):
                        half = 2 * s + kk // HK
                        pe.matmul(ps[:, s, :], whigh[:, half, w], hn[:, kk, :, :], start=kk == 0, stop=False,
                                  skip_group_check=True)
                        ins = pe.matmul(ps[:, s, T:2 * T], wlow[:, half, w], hn[:, kk, 0, :], start=False,
                                        stop=kk == KT - 1, skip_group_check=True)
                        if kk % HK == HK - 1 and (s == 0 or kk == KT - 1):
                            ins.then_inc(S["halves_multiplied"], s + 1)

            def tokens_body(n, kind):
                for s in range(CH):
                    for h in range(2):
                        pe.wait_ge(S["low_ready"], n * 8 + 2 * s + h + 1)
                        half = (2 * s + h) % 4
                        for j in range(2):
                            tok = slice(j * P, j * P + P)
                            if s == 0 and h == 0:
                                pe.wait_ge(S["chunks_evicted"], n * CH + 3 + j)
                            for k in range(2):
                                kk = 4 * s + 2 * h + k
                                w = slice(k * 512, k * 512 + 512)
                                for first, a, b in ((kk == 0, 0, whigh), (False, 0, wlow), (False, 1, whigh)):
                                    ins = pe.matmul(ps[:, 2 + j, :], hn[:, kk, a, tok], b[:, half, w], start=first,
                                                    stop=kk == KT - 1 and a == 1, skip_group_check=True)
                        ins.then_inc(S["halves_multiplied"], 1)

            def body(n, kind, q, i, pair, units, fresh=False):
                if kind in TOKENS:
                    return tokens_body(n, kind)
                if fresh:
                    fresh_half(n, kind)
                src = mid if kind[:3] in ("out", "dow") else hn
                kts = GROUPS[2] if "short" in kind else KT
                for s in range(2 if fresh else 0, CH):
                    pe.wait_ge(S["chunks_evicted"], n * CH + s + 1)
                    for h in range(2):
                        pe.wait_ge(S["low_ready"], n * 8 + 2 * s + h + 1)
                        half = (2 * s + h) % 4
                        for k in range(min(HK, kts - h * HK)):
                            kk = h * HK + k
                            if kind[:4] == "down":
                                if kk >= kts - 4 or kk % 4 == 0:
                                    first = q * GROUPS[0] + int(kind[4]) * FT
                                    pe.wait_ge(S["hidden_ready"], first + (kk + 1 if kk >= kts - 4 else kk + 4))
                            elif kind == "out1":
                                if s == 0 and kk in (12, 14):
                                    pe.wait_ge(S["s_low"], 6 + (kk - 12) // 2 + 1 + 2)
                            w = slice(k * P, k * P + P)
                            pe.matmul(ps[:, s, :], whigh[:, half, w], src[:, kk, :, :], start=kk == 0, stop=False,
                                      skip_group_check=True)
                            ins = pe.matmul(ps[:, s, T:2 * T], wlow[:, half, w], src[:, kk, 0, :], start=False,
                                            stop=kk == kts - 1, skip_group_check=True)
                        ins.then_inc(S["halves_multiplied"], 1)

            def between(name, c):
                if name == "start":
                    pe.sem_inc(S["halves_multiplied"], CREDIT)
                elif name == "norm":
                    pe.wait_ge(S["square_step"], 33 * c + 33)
                    pe.matmul(ps[:, 7, 0:T], ones[:, :], squares_sum, start=True, stop=True).then_inc(S["variance_ready"], 1)
                elif name == "lru":
                    pe.wait_ge(S["lru_w_loaded"], 16)
                    gw = flat(GW).rearrange("p (g n e) -> p g n e", g=2, n=LT)
                    for n in range(LT):
                        pe.wait_ge(S["conv_ready"], n + 1)
                        if n >= 2:
                            pe.wait_ge(S["lru_root_in"], n - 1)
                        pe.matmul(ps[:, 4 + n % 2, 0:T], gw[:, 0, n, :], XC[:, n, :], start=True, stop=True)
                        pe.matmul(ps[:, 4 + n % 2, T:2 * T], gw[:, 1, n, :], XC[:, n, :], start=True, stop=True)\
                          .then_inc(S["lru_gates_ready"], 1)
                elif name == "gates":
                    pe.wait_ge(S["gate_w_ready"], 1)
                    pe.wait_ge(S["lru_root_in"], LT)
                    for j in range(2):
                        for k in range(KT):
                            tok = slice(j * P, j * P + P)
                            pe.matmul(ps[:, 5, 16 * j:16 * j + 16], hn[:, k, 0, tok], wg[:, k, :, :], start=k == 0, stop=False,
                                      skip_group_check=True)
                            ins = pe.matmul(ps[:, 5, 16 * j + 8:16 * j + 16], hn[:, k, 1, tok], wg[:, k, 0, :], start=False,
                                            stop=k == KT - 1, skip_group_check=True)
                    ins.then_inc(S["gates_summed"], 1)
                    pe.wait_ge(S["gate_tokens"], 1)
                    for which in range(2):
                        for j in range(2):
                            ins = pe.matmul(ps[0:HM, 4, which * T + j * P:which * T + j * P + P], gtok[:, j, HM * which:HM * which + HM],
                                            ident[:, :], start=True, stop=True)
                    ins.then_inc(S["gate_rows"], 1)
                    pe.wait_ge(S["decay_rows"], 1)
                    for j in range(2):
                        ins = pe.matmul(ps[:, 6, HM * j:HM * j + HM], row(5)[:, j * P:j * P + P], ident[0:HM, 0:HM], start=True, stop=True)
                    ins.then_inc(S["gate_cols"], 1)
                elif name == "mlstm":
                    pe.wait_ge(S["chunks_evicted"], (IN0 + 10) * CH + CREDIT)
                    pe.wait_ge(S["gate_cols_read"], 1)

                    def head_row(h):
                        return ident[0:HM, h:h + 1].to_broadcast([HM, P])

                    def scores(h):
                        if h:
                            pe.wait_ge(S["m_scored"], h)
                            pe.wait_ge(S["m_floor"], h)
                        bank = 4 + h % 2
                        pe.matmul(ps[:, bank, 0:T], head_row(h), row(6), start=True, stop=False, skip_group_check=True)
                        pe.matmul(ps[:, bank, 0:P], ident[:, :], shut[:, 0, :], start=False, stop=True, skip_group_check=True)
                        pe.matmul(ps[:, bank, T:T + P], head_row(h), row(6)[:, P:T], start=True, stop=False, skip_group_check=True)
                        pe.matmul(ps[:, bank, T:T + P], ident[:, :], shut[:, 0, :], start=False, stop=True, skip_group_check=True)
                        pe.matmul(ps[:, 3 + 4 * (h // 2), (h % 2) * T:(h % 2) * T + T], head_row(h), row(7), start=True, stop=True)
                        q, k = work[:, h, :], work[:, 4 + h, :]
                        pe.matmul(ps[:, 6, 0:T], k[:, 0:P], q, start=True, stop=True)
                        pe.matmul(ps[:, 6, T:T + P], k[:, P:T], q[:, P:T], start=True, stop=True).then_inc(S["m_scores_raw"], 1)

                    def causal(dst, lhs, score):
                        pe.matmul(dst, lhs[0], score[:, 0:T], start=True, stop=False, skip_group_check=True)
                        return pe.matmul(dst[:, P:T], lhs[1], score[:, T:T + P], start=False, stop=True, skip_group_check=True)

                    def products(h):
                        pe.wait_ge(S["m_scored"], h + 1)
                        if h:
                            pe.wait_ge(S["m_normed"], h)
                        causal(ps[:, 2, (h % 2) * T:(h % 2) * T + T], [ones[:, :]] * 2, m_score(h))
                        for v in range(2):
                            col = h * DV + v * P
                            ins = causal(ps[:, h % 2, v * T:v * T + T], [t[:, col:col + P] for t in vtok], m_score(h))
                        ins.then_inc(S["m_products"], 1)

                    def meansq(h):
                        pe.wait_ge(S["m_squared"], h + 1)
                        pe.wait_ge(S["m_floor"], h // 2 * 2 + 2)
                        dst = ps[:, 3 + 4 * (h // 2), (h % 2) * T:(h % 2) * T + T]
                        sq = m_score(h)
                        pe.matmul(dst, ones[:, :], sq[:, 0:T], start=True, stop=False, skip_group_check=True)
                        pe.matmul(dst, ones[:, :], sq[:, T:2 * T], start=False, stop=True, skip_group_check=True)\
                          .then_inc(S["m_meansq"], 1)

                    scores(0)
                    scores(1)
                    products(0)
                    for h in range(2, HM):
                        scores(h)
                        meansq(h - 2)
                        products(h - 1)
                    meansq(2)
                    products(3)
                    meansq(3)
                    pe.wait_ge(S["m_roots"], 1)
                    pe.wait_ge(S["mixer_low"], 2)
                elif name == "scores":
                    pe.wait_ge(S["chunks_evicted"], (c * 3 + (IN1 + 2)) * CH + CREDIT)
                    pe.wait_ge(S["s_low"], c * 2 + 2)
                    for w in range(2):
                        for h in (2 * w, 2 * w + 1):
                            q, k = work[:, h, :], work[:, 4 + h, :]
                            pe.matmul(ps[:, 4 + h, 0:T], k[:, 0:P], q, start=True, stop=False, skip_group_check=True)
                            ins = pe.matmul(ps[:, 4 + h, T:T + P], k[:, P:T], q[:, P:T], start=False, stop=False,
                                            skip_group_check=True)
                        ins.then_inc(S["s_scores"], 1)
                elif name == "sums":
                    for w in range(2):
                        pe.wait_ge(S["s_masked"], (c * 2 + w) * 4 + 4)
                        for h in range(2):
                            z = ps[:, 4 + 2 * w + h, :]
                            soft = s_soft(w)[:, h, :]
                            pe.matmul(z[:, 0:T], tri[:, :], soft[:, 0:T], start=False, stop=False, skip_group_check=True)
                            pe.matmul(z[:, P:T], minus[:, :], soft[:, T:T + P], start=False, stop=False, skip_group_check=True)
                            pe.matmul(z[:, T:T + P], tri[:, :], soft[:, T:T + P], start=False, stop=False, skip_group_check=True)
                            for block in (slice(0, P), slice(T, T + P)):
                                ins = pe.matmul(z[:, block], ident[:, :], shut[:, 1, :], start=False, stop=True, skip_group_check=True)
                        ins.then_inc(S["s_logits"], 1)
                elif name == "values":
                    pe.wait_ge(S["chunks_evicted"], (c * 3 + (IN1 + 3)) * CH + CREDIT)
                    for w in range(2):
                        pe.wait_ge(S["s_probs"], c * 2 + w + 1)
                        for h in range(2):
                            dst = ps[:, 4 + 2 * w, h * T:h * T + T]
                            probs = s_tmp(w)[:, h, :]
                            col = (2 * w + h) * P
                            pe.matmul(dst, s_vtok[:, 0, col:col + P], probs[:, 0:T], start=True, stop=False, skip_group_check=True)
                            ins = pe.matmul(dst[:, P:T], s_vtok[:, 1, col:col + P], probs[:, T:T + P], start=False, stop=True,
                                            skip_group_check=True)
                        ins.then_inc(S["s_out"], 1)

            run_stream(pe, body, between)


def kernel(x, c, ada_w, ada_b, norm_g, final_g, ffn_w1, ffn_w3, ffn_w2, ab_w_in, ab_w_out, lru_conv_w, lru_conv_b,
           lru_gate_w, lru_gate_b, lru_lambda, mlstm_gate_b, mlstm_norm_g, sb_w_qkv, sb_w_out):
    import numpy as np
    import concourse.bacc as bacc
    from concourse.bass_utils import run_bass_kernel_spmd as run

    def chunks(w):
        k, n = w.shape
        return w.reshape(k // P, P, n // P, P).transpose(2, 1, 0, 3).reshape(n // P, P, k)

    x, ada_w, w_in = np.asarray(x), np.asarray(ada_w), np.asarray(ab_w_in)[0]
    w1, w3, w2 = (np.asarray(w) for w in (ffn_w1, ffn_w3, ffn_w2))
    wts = np.zeros((BODIES * CH, P, D), w_in.dtype)
    at = [0]

    def put(c):
        wts[at[0]:at[0] + c.shape[0], :, :c.shape[2]] = c
        at[0] += c.shape[0]

    def put_ffn(layer):
        first = 0
        for n in GROUPS:
            cols = slice(first * P, (first + n) * P)
            put(np.stack([chunks(w1[layer][:, cols]), chunks(w3[layer][:, cols])], axis=1).reshape(2 * n, P, D))
            put(chunks(w2[layer][cols]))
            first += n

    def token_chunks(w):
        k, n = w.shape
        return w.reshape(k // 512, 4, P, n // 512, 512).transpose(3, 0, 2, 1, 4).reshape(n * k // (P * D), P, D)

    put(chunks(w_in[:, :3072]))
    put(token_chunks(w_in[:, 3072:4096]))
    put(chunks(w_in[:, 4096:5120]))
    put(chunks(np.asarray(ab_w_out)[0]))
    put_ffn(0)
    qkv = np.asarray(sb_w_qkv)[0]
    for g in range(4):
        for j, layout in enumerate((chunks, chunks, token_chunks)):
            put(layout(qkv[:, j * D + g * 512:j * D + g * 512 + 512]))
    put(chunks(np.asarray(sb_w_out)[0]))
    put_ffn(1)

    def cols(a, lead):
        a = np.asarray(a).reshape(lead, -1, P)
        return np.ascontiguousarray(a.transpose(2, 0, 1))

    ada = ada_w.reshape(4, D, 3 * D).transpose(0, 2, 1).reshape(12, KT, P, D)
    data = {
        "xT": np.ascontiguousarray(x[0].T.reshape(KT, P, T).transpose(1, 0, 2)),
        "c_row": np.asarray(c).reshape(1, D),
        "wts": wts,
        "ada": np.concatenate([ada[:2].transpose(1, 0, 2, 3).reshape(2 * KT, P, D), ada[2:].reshape(10 * KT, P, D)]),
        "ada_b": cols(ada_b, 1)[:, 0, :],
        "norm_g": cols(np.concatenate([np.asarray(norm_g).reshape(4, D), np.asarray(final_g).reshape(1, D)]), 5),
        "wgate": np.ascontiguousarray(w_in[:, 5120:].reshape(KT, P, 8).transpose(1, 0, 2)),
        "conv": np.ascontiguousarray(np.concatenate([np.asarray(lru_conv_w)[0], np.asarray(lru_conv_b)]).reshape(5, LT, P).transpose(2, 1, 0)),
        "lru_w": np.ascontiguousarray(np.asarray(lru_gate_w)[0].transpose(2, 0, 1, 3)).reshape(P, 2 * LT * P),
        "lru_b": cols(np.asarray(lru_gate_b)[0], 2),
        "lam": cols(lru_lambda, 1)[:, 0, :],
        "gate_b": np.ascontiguousarray(np.asarray(mlstm_gate_b)[0].T),
        "mnorm_g": cols(mlstm_norm_g, 1)[:, 0, :],
    }
    data = {name: np.ascontiguousarray(a) for name, a in data.items()}
    nc = bacc.Bacc("TRN2", target_bir_lowering=False, num_devices=1)
    args = {name: nc.dram_tensor(name + "_dram", a.shape, mybir.dt.from_np(a.dtype), kind="ExternalInput").ap()
            for name, a in data.items()}
    out = nc.dram_tensor("out_dram", (P, KT, T), F32, kind="ExternalOutput").ap()
    bass_trunk(nc, out=out, **args)
    r = run(nc, [{name + "_dram": a for name, a in data.items()}], core_ids=[0])
    return r.results[0]["out_dram"].transpose(2, 1, 0).reshape(1, T, D)
```
